# Optimizing a Trainium2 kernel written in Bass

```python
import math
import jax, jax.numpy as jnp
from jax import lax
import numpy as np

D_MODEL = 2048
BATCH = 1
SEQ = 256
DEPTH = 1

ATTN_HEAD_DIM = 128
ATTN_HEADS = D_MODEL // ATTN_HEAD_DIM
ATTN_WIDTH = ATTN_HEADS * ATTN_HEAD_DIM
MOBA_BLOCK = 256
MOBA_TOPK = 3
QUERY_CHUNK = 32
SSM_EXPAND = 2
SSM_INNER = SSM_EXPAND * D_MODEL
SSM_HEAD_DIM = 64
SSM_HEADS = SSM_INNER // SSM_HEAD_DIM
SSM_GROUPS = 8
SSM_STATE = 128
SSM_CONV = 4
SSM_CHUNK = 128
SSM_CONV_DIM = SSM_INNER + 2 * SSM_GROUPS * SSM_STATE
N_BRANCHES = 2
D_FF = 4 * D_MODEL
IN_SPLITS = (ATTN_WIDTH, ATTN_WIDTH, ATTN_WIDTH, SSM_INNER, SSM_CONV_DIM, SSM_HEADS, N_BRANCHES * D_MODEL)
IN_COLS = 3 * ATTN_WIDTH + SSM_INNER + SSM_CONV_DIM + SSM_HEADS + N_BRANCHES * D_MODEL
EPS = 1e-6
NEG_INF = -1e30

kernel_name = "hybrid_moba_ssd_gated_block"

def rms_norm(x, w):
    xf = x.astype(jnp.float32)
    y = xf * lax.rsqrt(jnp.mean(jnp.square(xf), axis=-1, keepdims=True) + EPS)
    return (y * w.astype(jnp.float32)).astype(x.dtype)

def alibi_slopes(n_heads):
    return jnp.exp2(-8.0 * jnp.arange(1, n_heads + 1, dtype=jnp.float32) / n_heads)

def moba_attention(q, k, v, slopes):
    bsz, n_h, seq, dh = q.shape
    nb = -(-seq // MOBA_BLOCK)
    pad = nb * MOBA_BLOCK - seq
    kp = jnp.pad(k, ((0, 0), (0, 0), (0, pad), (0, 0)))
    vp = jnp.pad(v, ((0, 0), (0, 0), (0, pad), (0, 0)))
    k_blocks = kp.reshape(bsz, n_h, nb, MOBA_BLOCK, dh)
    v_blocks = vp.reshape(bsz, n_h, nb, MOBA_BLOCK, dh)
    k_mean = jnp.mean(k_blocks.astype(jnp.float32), axis=3)
    n_sel = max(1, min(MOBA_TOPK, nb - 1))
    scale = dh ** -0.5
    gather_blocks = jax.vmap(jax.vmap(lambda blocks, idx: blocks[idx]))
    blk_pos = jnp.arange(MOBA_BLOCK)

    def chunk_fn(c):
        q0 = c * QUERY_CHUNK
        qc = lax.dynamic_slice_in_dim(q, q0, QUERY_CHUNK, axis=2)
        t = q0 + jnp.arange(QUERY_CHUNK)
        own = q0 // MOBA_BLOCK
        gate = jnp.einsum('bhqd,bhnd->bhqn', qc.astype(jnp.float32), k_mean)
        gate = jnp.where(jnp.arange(nb) < own, gate, NEG_INF)
        _, sel = lax.top_k(gate, n_sel)
        sel_valid = sel < own
        kg = gather_blocks(k_blocks, sel)
        vg = gather_blocks(v_blocks, sel)
        s_sel = jnp.einsum('bhqd,bhqjkd->bhqjk', qc, kg).astype(jnp.float32) * scale
        pos_sel = sel[..., None] * MOBA_BLOCK + blk_pos
        dist_sel = (t[:, None, None] - pos_sel).astype(jnp.float32)
        s_sel = s_sel - slopes[:, None, None, None] * dist_sel
        s_sel = jnp.where(sel_valid[..., None], s_sel, NEG_INF)
        ko = lax.dynamic_slice_in_dim(kp, own * MOBA_BLOCK, MOBA_BLOCK, axis=2)
        vo = lax.dynamic_slice_in_dim(vp, own * MOBA_BLOCK, MOBA_BLOCK, axis=2)
        s_own = jnp.einsum('bhqd,bhkd->bhqk', qc, ko).astype(jnp.float32) * scale
        dist_own = t[:, None] - (own * MOBA_BLOCK + blk_pos)[None, :]
        s_own = jnp.where(dist_own >= 0, s_own - slopes[:, None, None] * dist_own.astype(jnp.float32), NEG_INF)
        logits = jnp.concatenate([s_sel.reshape(bsz, n_h, QUERY_CHUNK, n_sel * MOBA_BLOCK), s_own], axis=-1)
        p = jax.nn.softmax(logits, axis=-1)
        p_sel = p[..., :n_sel * MOBA_BLOCK].reshape(bsz, n_h, QUERY_CHUNK, n_sel, MOBA_BLOCK)
        p_own = p[..., n_sel * MOBA_BLOCK:]
        out = (jnp.einsum('bhqjk,bhqjkd->bhqd', p_sel, vg.astype(jnp.float32))
               + jnp.einsum('bhqk,bhkd->bhqd', p_own, vo.astype(jnp.float32)))
        return out.astype(q.dtype)

    outs = lax.map(chunk_fn, jnp.arange(seq // QUERY_CHUNK))
    return outs.transpose(1, 2, 0, 3, 4).reshape(bsz, n_h, seq, dh)

def causal_depthwise_conv(u, w, b):
    width = w.shape[0]
    out = lax.conv_general_dilated(
        u, w[:, None, :], window_strides=(1,), padding=[(width - 1, 0)],
        dimension_numbers=('NWC', 'WIO', 'NWC'), feature_group_count=u.shape[-1])
    return out + b

def ssd_chunked(x, dt, a, b_in, c_in):
    bsz, seq, n_h, p = x.shape
    g, n = b_in.shape[2], b_in.shape[3]
    hg = n_h // g
    ln = SSM_CHUNK
    nc = seq // ln
    xf = (x.astype(jnp.float32) * dt[..., None]).reshape(bsz, nc, ln, g, hg, p)
    la = (dt * a).reshape(bsz, nc, ln, g, hg)
    a_cum = jnp.cumsum(la, axis=2)
    bc = b_in.astype(jnp.float32).reshape(bsz, nc, ln, g, n)
    cc = c_in.astype(jnp.float32).reshape(bsz, nc, ln, g, n)
    seg = a_cum[:, :, :, None] - a_cum[:, :, None]
    causal = jnp.tril(jnp.ones((ln, ln), dtype=bool))[None, None, :, :, None, None]
    decay = jnp.exp(jnp.where(causal, seg, -jnp.inf))
    cb = jnp.einsum('bclgn,bcsgn->bclsg', cc, bc)
    y_diag = jnp.einsum('bclsgh,bcsghp->bclghp', cb[..., None] * decay, xf)
    decay_to_end = jnp.exp(a_cum[:, :, -1:] - a_cum)
    states = jnp.einsum('bclgn,bclghp->bcghpn', bc, xf * decay_to_end[..., None])
    chunk_decay = jnp.exp(a_cum[:, :, -1])

    def step(h, inp):
        st, dcy = inp
        return h * dcy[..., None, None] + st, h

    h0 = jnp.zeros((bsz, g, hg, p, n), jnp.float32)
    _, prev = lax.scan(step, h0, (states.swapaxes(0, 1), chunk_decay.swapaxes(0, 1)))
    prev = prev.swapaxes(0, 1)
    y_off = jnp.einsum('bclgn,bcghpn->bclghp', cc, prev) * jnp.exp(a_cum)[..., None]
    return (y_diag + y_off).reshape(bsz, seq, n_h, p)

def mamba2_branch(z, xbc, dt_raw, conv_w, conv_b, dt_bias, a_log, d_skip, norm_w):
    bsz, seq, _ = xbc.shape
    xbc = jax.nn.silu(causal_depthwise_conv(xbc, conv_w, conv_b))
    xs = xbc[..., :SSM_INNER].reshape(bsz, seq, SSM_HEADS, SSM_HEAD_DIM)
    b_in = xbc[..., SSM_INNER:SSM_INNER + SSM_GROUPS * SSM_STATE].reshape(bsz, seq, SSM_GROUPS, SSM_STATE)
    c_in = xbc[..., SSM_INNER + SSM_GROUPS * SSM_STATE:].reshape(bsz, seq, SSM_GROUPS, SSM_STATE)
    dt = jax.nn.softplus(dt_raw.astype(jnp.float32) + dt_bias.astype(jnp.float32))
    a = -jnp.exp(a_log.astype(jnp.float32))
    y = ssd_chunked(xs, dt, a, b_in, c_in) + xs.astype(jnp.float32) * d_skip.astype(jnp.float32)[:, None]
    y = y.reshape(bsz, seq, SSM_INNER) * jax.nn.silu(z.astype(jnp.float32))
    yg = y.reshape(bsz, seq, SSM_GROUPS, SSM_INNER // SSM_GROUPS)
    yg = yg * lax.rsqrt(jnp.mean(jnp.square(yg), axis=-1, keepdims=True) + EPS)
    y = yg.reshape(bsz, seq, SSM_INNER) * norm_w.astype(jnp.float32)
    return y.astype(z.dtype)

def setup_inputs(seed: int = 0) -> dict:
    key = jax.random.key(seed)
    ks = jax.random.split(key, 18)
    f32 = jnp.float32

    def normal(k, shape, scale):
        return jax.random.normal(k, shape, f32) * scale

    x = normal(ks[0], (BATCH, SEQ, D_MODEL), 1.0)
    mix_norm_w = 1.0 + normal(ks[1], (DEPTH, D_MODEL), 0.02)
    w_in = normal(ks[2], (DEPTH, D_MODEL, IN_COLS), D_MODEL ** -0.5)
    q_norm_w = 1.0 + normal(ks[3], (DEPTH, ATTN_HEAD_DIM), 0.02)
    k_norm_w = 1.0 + normal(ks[4], (DEPTH, ATTN_HEAD_DIM), 0.02)
    conv_w = normal(ks[5], (DEPTH, SSM_CONV, SSM_CONV_DIM), SSM_CONV ** -0.5)
    conv_b = normal(ks[6], (DEPTH, SSM_CONV_DIM), 0.01)
    dt0 = jnp.exp(jax.random.uniform(ks[7], (DEPTH, SSM_HEADS), f32, math.log(1e-3), math.log(1e-1)))
    dt_bias = dt0 + jnp.log(-jnp.expm1(-dt0))
    a_log = jnp.log(jax.random.uniform(ks[8], (DEPTH, SSM_HEADS), f32, 1.0, 16.0))
    d_skip = 1.0 + normal(ks[9], (DEPTH, SSM_HEADS), 0.02)
    ssm_norm_w = 1.0 + normal(ks[10], (DEPTH, SSM_INNER), 0.02)
    w_attn_out = normal(ks[11], (DEPTH, ATTN_WIDTH, D_MODEL), ATTN_WIDTH ** -0.5)
    w_ssm_out = normal(ks[12], (DEPTH, SSM_INNER, D_MODEL), SSM_INNER ** -0.5)
    w_out = normal(ks[13], (DEPTH, D_MODEL, D_MODEL), D_MODEL ** -0.5)
    mlp_norm_w = 1.0 + normal(ks[14], (DEPTH, D_MODEL), 0.02)
    w_up = normal(ks[15], (DEPTH, D_MODEL, D_FF), D_MODEL ** -0.5)
    w_down = normal(ks[16], (DEPTH, D_FF, D_MODEL), D_FF ** -0.5)
    return {"x": x, "mix_norm_w": mix_norm_w, "w_in": w_in, "q_norm_w": q_norm_w, "k_norm_w": k_norm_w,
            "conv_w": conv_w, "conv_b": conv_b, "dt_bias": dt_bias, "a_log": a_log, "d_skip": d_skip,
            "ssm_norm_w": ssm_norm_w, "w_attn_out": w_attn_out, "w_ssm_out": w_ssm_out, "w_out": w_out,
            "mlp_norm_w": mlp_norm_w, "w_up": w_up, "w_down": w_down}

def reference(x, mix_norm_w, w_in, q_norm_w, k_norm_w, conv_w, conv_b, dt_bias, a_log, d_skip,
              ssm_norm_w, w_attn_out, w_ssm_out, w_out, mlp_norm_w, w_up, w_down):
    bsz, seq, _ = x.shape
    slopes = alibi_slopes(ATTN_HEADS)
    split_points = []
    acc = 0
    for width in IN_SPLITS[:-1]:
        acc += width
        split_points.append(acc)
    h = x
    for layer in range(DEPTH):
        hn = rms_norm(h, mix_norm_w[layer])
        proj = hn @ w_in[layer]
        q, k, v, z, xbc, dt_raw, gate_logits = jnp.split(proj, split_points, axis=-1)
        q = rms_norm(q.reshape(bsz, seq, ATTN_HEADS, ATTN_HEAD_DIM), q_norm_w[layer]).transpose(0, 2, 1, 3)
        k = rms_norm(k.reshape(bsz, seq, ATTN_HEADS, ATTN_HEAD_DIM), k_norm_w[layer]).transpose(0, 2, 1, 3)
        v = v.reshape(bsz, seq, ATTN_HEADS, ATTN_HEAD_DIM).transpose(0, 2, 1, 3)
        attn = moba_attention(q, k, v, slopes).transpose(0, 2, 1, 3).reshape(bsz, seq, ATTN_WIDTH)
        y_attn = attn @ w_attn_out[layer]
        ssm = mamba2_branch(z, xbc, dt_raw, conv_w[layer], conv_b[layer], dt_bias[layer], a_log[layer],
                            d_skip[layer], ssm_norm_w[layer])
        y_ssm = ssm @ w_ssm_out[layer]
        gates = jax.nn.sigmoid(gate_logits.astype(jnp.float32)).astype(h.dtype)
        g_attn, g_ssm = gates[..., :D_MODEL], gates[..., D_MODEL:]
        h = h + (g_attn * y_attn + g_ssm * y_ssm) @ w_out[layer]
        u = rms_norm(h, mlp_norm_w[layer]) @ w_up[layer]
        h = h + jnp.square(jax.nn.relu(u)) @ w_down[layer]
    return h


_drawn_inputs = setup_inputs


def setup_inputs(seed=0):
    import zlib

    import numpy as np

    out = dict(_drawn_inputs(seed))
    spreads = {}
    factors = {'mix_norm_w': 3.267,
     'q_norm_w': 8.0,
     'k_norm_w': 8.0,
     'conv_b': 7.886,
     'd_skip': 200.0,
     'ssm_norm_w': 16.128,
     'mlp_norm_w': 10.126}
    for name, (base, spread) in spreads.items():
        noise = np.random.default_rng([zlib.crc32(name.encode()), seed]).standard_normal(out[name].shape)
        drawn = base * np.exp(spread * noise) if base else spread * noise
        out[name] = __import__('jax').numpy.asarray(drawn.astype(out[name].dtype))
    for name, factor in factors.items():
        out[name] = (out[name] * factor).astype(out[name].dtype)
    return out
```

```python
import concourse.bass as bass
from concourse import mybir
from contextlib import ExitStack

D = 2048
T = 256
P = 128
NTOK = T // P
HD = 128
NH = D // HD
INNER = 2 * D
SHD = 64
SNH = INNER // SHD
GROUPS = 8
HG = SNH // GROUPS
GW = INNER // GROUPS
NST = 128
CONV_DIM = INNER + 2 * GROUPS * NST
FF = 4 * D
EPS = 1e-6
Q0, K0, V0 = 0, D, 2 * D
Z0 = 3 * D
XBC0 = Z0 + INNER
DT0 = XBC0 + CONV_DIM
GATE0 = DT0 + SNH

COLS = 512
KT = D // P
UK = 2
US = KT // UK
SLOTS = 4
LEAD = 3

B_QKV = 0
B_CONV = 12
B_SSD = 24
B_GATE = 40
B_SSM = 44
B_OUT = 52
B_MLP = 56


def build(nc, x, mix_norm_w, w_in, q_norm_w, k_norm_w, conv_w, conv_b, dt_bias, a_log, d_skip, ssm_norm_w,
          w_attn_out, w_ssm_out, w_out, mlp_norm_w, w_up, w_down, out):
    f32 = mybir.dt.float32
    f32r = mybir.dt.float32r
    i32 = mybir.dt.int32
    ALU = mybir.AluOpType
    ACT = mybir.ActivationFunctionType
    AX = mybir.AxisListType

    x, w_in, w_attn_out, w_ssm_out = x[0], w_in[0], w_attn_out[0], w_ssm_out[0]
    w_out, w_up, w_down, out = w_out[0], w_up[0], w_down[0], out[0]

    ctx = ExitStack()
    with ctx:
        BASE = 16512
        KB = 1024
        at = {"RAW": 0, "HI": 16 * KB, "LO": 32 * KB, "A": 48 * KB, "B": 80 * KB, "C": 112 * KB, "D": 144 * KB,
              "E": 164 * KB, "W": 180 * KB}

        def sb(name, region, off, shape, dt=f32):
            return nc.alloc_sbuf_tensor_at(name, shape, dt, offset=BASE + at[region] + off)

        raw = [sb(f"raw{s}", "RAW", 4096 * s, [P, UK, COLS]) for s in range(SLOTS)]
        whi = [sb(f"whi{s}", "HI", 4096 * s, [P, UK, COLS], f32r) for s in range(SLOTS)]
        wlo = [sb(f"wlo{s}", "LO", 4096 * s, [P, UK, COLS], f32r) for s in range(SLOTS)]
        xT_hi = sb("xT_hi", "A", 0, [P, KT, T], f32r)
        xT_lo = sb("xT_lo", "A", 16 * KB, [P, KT, T], f32r)
        gT_hi = sb("gT_hi", "A", 0, [P, KT, T], f32r)
        gT_lo = sb("gT_lo", "A", 16 * KB, [P, KT, T], f32r)
        aT_hi = sb("aT_hi", "B", 0, [P, KT, T], f32r)
        aT_lo = sb("aT_lo", "B", 16 * KB, [P, KT, T], f32r)
        sT_lo = sb("sT_lo", "B", 0, [P, 2 * KT, T], f32r)
        hT_hi = sb("hT_hi", "B", 0, [P, KT, T], f32r)
        hT_lo = sb("hT_lo", "B", 16 * KB, [P, KT, T], f32r)
        q_st = sb("q_st", "C", 0, [P, NTOK, COLS])
        k_st = sb("k_st", "C", 4 * KB, [P, NTOK, COLS])
        v_st = sb("v_st", "C", 8 * KB, [P, NTOK, COLS])
        sq = sb("sq", "C", 12 * KB, [P, 8, HD])
        qT = sb("qT", "C", 16 * KB, [P, 4, T])
        kT = sb("kT", "C", 20 * KB, [P, 4, T])
        prob = sb("prob", "C", 24 * KB, [P, 3 * P])
        probT = sb("probT", "C", 24 * KB + 1536, [P, 3 * P])
        dist = sb("dist", "C", 24 * KB + 3072, [P, 3 * P])
        dist_i = sb("dist_i", "C", 24 * KB + 4608, [P, 3 * P], i32)
        xs = sb("xs", "C", 0, [P, GROUPS, NTOK, GW])
        sT_hi = sb("sT_hi", "C", 0, [P, 2 * KT, T], f32r)
        fT_hi = sb("fT_hi", "C", 0, [P, KT, T], f32r)
        fT_lo = sb("fT_lo", "C", 16 * KB, [P, KT, T], f32r)
        dtw = sb("dtw", "D", 0, [P, KT, SNH])
        dtw_hi = sb("dtw_hi", "D", 4 * KB, [P, KT, SNH], f32r)
        dtw_lo = sb("dtw_lo", "D", 8 * KB, [P, KT, SNH], f32r)
        prow = sb("prow", "D", 12 * KB, [P, 3, P])
        BT = sb("BT", "D", 0, [P, GROUPS, T])
        CT = sb("CT", "D", 8 * KB, [P, GROUPS, T])
        Btok = sb("Btok", "D", 16 * KB, [P, GROUPS * NST])
        sgate = sb("sgate", "D", 0, [P, NTOK, D])
        x_in = sb("x_in", "E", 0, [P, NTOK, D])
        c_st = [sb(f"c_st{i}", "E", 4 * KB * i, [P, NTOK, COLS]) for i in range(2)]
        cacc = sb("cacc", "E", 8 * KB, [P, 4, T])
        cT = sb("cT", "E", 12 * KB, [P, 4, T])
        merged = sb("merged", "E", 0, [P, NTOK, D])
        h = sb("h", "E", 0, [P, NTOK, D])
        lm = sb("lm", "W", 0, [P, HG, P])
        zs = sb("zs", "W", 4 * KB, [P, NTOK, COLS])
        xf = sb("xf", "W", 8 * KB, [P, HG, SHD])
        xd = sb("xd", "W", 10 * KB, [P, HG, SHD])
        prev = sb("prev", "W", 12 * KB, [P, GW])
        yoff = sb("yoff", "W", 14 * KB, [P, HG, SHD])
        BTg = sb("BTg", "W", 16 * KB, [P, T])
        CTg = sb("CTg", "W", 17 * KB, [P, T])
        Btg = sb("Btg", "W", 18 * KB, [P, NST])
        cbm = sb("cbm", "W", 18 * KB + 512, [P, P])
        y_st = [sb(f"y_st{i}", "W", 4 * KB * i, [P, NTOK, GW]) for i in range(2)]
        s_half = sb("s_half", "W", 0, [P, NTOK, COLS])
        m_st = sb("m_st", "W", 8 * KB, [P, NTOK, COLS])
        r_st = sb("r_st", "W", 0, [P, NTOK, COLS])
        woff = [19 * KB]

        def small(name, shape, dt=f32):
            n = 4
            for s in shape[1:]:
                n *= s
            t = sb(name, "W", woff[0], shape, dt)
            woff[0] += -(-n // 32) * 32
            return t

        ident = small("ident", [P, P])
        tri = small("tri", [P, P])
        strict = small("strict", [P, P])
        NPAR = 306
        par = small("par", [P, NPAR])
        MIX_C, MLP_C, SSM_C, CB_C, QN_C, KN_C, CW_C = 0, 16, 32, 64, 112, 113, 114
        negslope = small("negslope", [P, 4])
        neghalf = small("neghalf", [P, 8])
        ssum = small("ssum", [P, 8])
        rqk = small("rqk", [P, 8])
        xss = small("xss", [P, 2])
        rstd1 = small("rstd1", [P, 2])
        negmax = small("negmax", [P, 2])
        psum_ = small("esum", [P, 2])
        pinv = small("pinv", [P, 2])
        dbias = small("dbias", [P, SNH])
        alog = small("alog", [P, SNH])
        dskip = small("dskip", [P, SNH])
        dt_ = small("dt", [P, NTOK, SNH])
        la = small("la", [P, NTOK, SNH])
        dtd = small("dtd", [P, SNH])
        eac = small("eac", [P, SNH])
        cw = small("cw", [P, 4, 4])
        cb = small("cb", [P, 4])
        gss = small("gss", [P, 2])
        grs = small("grs", [P, 2])
        sw = [small(f"sw{i}", [P, 4]) for i in range(2)]
        hss = small("hss", [P, NTOK, 4])
        hs2 = small("hs2", [P, 2])
        rstd2 = small("rstd2", [P, 2])
        assert BASE + at["W"] + woff[0] <= 229344, (woff[0], 229344 - BASE - at["W"])
        dts = [sb(f"dts{i}", "C", 12 * KB + 512 * i, [P, NTOK, SNH]) for i in range(8)]
        xjunk = [sb(f"xjunk{t}", "B", 8 * KB * t, [P, D]) for t in range(NTOK)]

        ps = [ctx.enter_context(nc.psum_tensor(f"ps{i}", [P, 512], f32)) for i in range(8)]
        SETS = [(ps[0], ps[1]), (ps[2], ps[3]), (ps[4], ps[5])]

        def sem(name):
            return ctx.enter_context(nc.semaphore(name))

        raw_in = [sem(f"raw_in{s}") for s in range(SLOTS)]
        hi_ready = sem("hi_ready")
        lo_ready = sem("lo_ready")
        unit_used = sem("unit_used")
        set_free = [sem(f"set_free{k}") for k in range(3)]
        x_loaded = [sem(f"x_loaded{c}") for c in range(4)]
        par_loaded = sem("par_loaded")
        row_loaded = sem("row_loaded")
        dtw_loaded = sem("dtw_loaded")
        const_step = sem("const_step")
        const_ready = sem("const_ready")
        par_T = sem("par_T")
        par_ready = sem("par_ready")
        x_T = sem("x_T")
        xT_hi_done = sem("xT_hi_done")
        xT_lo_done = sem("xT_lo_done")
        xsq_done = sem("xsq_done")
        xms_done = sem("xms_done")
        rstd1_ready = sem("rstd1_ready")
        dtw_hi_done = sem("dtw_hi_done")
        dtw_lo_done = sem("dtw_lo_done")
        dt_mm = sem("dt_mm")
        dt_v = sem("dt_v")
        dt_s = sem("dt_s")
        dec_mm = sem("dec_mm")
        dec_exp = sem("dec_exp")
        dt_ready = sem("dt_ready")
        qk_sq = sem("qk_sq")
        qk_sum = sem("qk_sum")
        qk_ms = sem("qk_ms")
        qk_rstd = sem("qk_rstd")
        qk_normed = sem("qk_normed")
        qk_T = sem("qk_T")
        qkT_ready = sem("qkT_ready")
        scores = sem("scores")
        biased = sem("biased")
        maxed = sem("maxed")
        expd = sem("expd")
        inv_done = sem("inv_done")
        normed = sem("normed")
        p_T = sem("p_T")
        probT_ready = sem("probT_ready")
        pv = sem("pv")
        aT_hi_done = sem("aT_hi_done")
        aT_lo_done = sem("aT_lo_done")
        slope_done = sem("slope_done")
        c_T = sem("c_T")
        c_par = sem("c_par")
        c_first = sem("c_first")
        c_tap = sem("c_tap")
        c_silu = sem("c_silu")
        c_back = sem("c_back")
        c_out = sem("c_out")
        g_copied = sem("g_copied")
        lm_ready = sem("lm_ready")
        xf_ready = sem("xf_ready")
        skip_ready = sem("skip_ready")
        seg_mm = sem("seg_mm")
        cb_mm = sem("cb_mm")
        dec_done = sem("dec_done")
        cbm_done = sem("cbm_done")
        M_ready = sem("M_ready")
        st_mm = sem("st_mm")
        prev_ready = sem("prev_ready")
        off_mm = sem("off_mm")
        y_mm = sem("y_mm")
        yd_done = sem("yd_done")
        yo_done = sem("yo_done")
        y_done = sem("y_done")
        z_sig = sem("z_sig")
        z_done = sem("z_done")
        yz_done = sem("yz_done")
        ysq_done = sem("ysq_done")
        yms_done = sem("yms_done")
        yrs_done = sem("yrs_done")
        yfin = sem("yfin")
        agate_done = sem("agate_done")
        attn_merged = sem("attn_merged")
        sgate_done = sem("sgate_done")
        y_copied = sem("y_copied")
        y_T = sem("y_T")
        sT_hi_done = sem("sT_hi_done")
        sT_lo_done = sem("sT_lo_done")
        half_done = sem("half_done")
        m_step = sem("m_step")
        m_ready = sem("m_ready")
        m_T = sem("m_T")
        gT_hi_done = sem("gT_hi_done")
        gT_lo_done = sem("gT_lo_done")
        x_again = sem("x_again")
        h_sq = sem("h_sq")
        h_T = sem("h_T")
        hT_hi_done = sem("hT_hi_done")
        hT_lo_done = sem("hT_lo_done")
        hsum_done = sem("hsum_done")
        hms_done = sem("hms_done")
        rstd2_ready = sem("rstd2_ready")
        relu_done = sem("relu_done")
        r_ready = sem("r_ready")
        r_T = sem("r_T")
        fT_hi_done = sem("fT_hi_done")
        fT_lo_done = sem("fT_lo_done")
        stored = sem("stored")

        def fp(ap):
            return ap.bitcast(f32)

        def over(ap, axis, n):
            a = ap.unsqueeze(axis)
            shape = list(a.shape)
            shape[axis] = n
            return a.to_broadcast(shape)

        def heads(ap, n):
            return ap.rearrange("p (h d) -> p h d", h=n)

        def later(n):
            return not (isinstance(n, int) and n == 0)

        block = ctx.enter_context(nc.Block())

        @block.sync
        def _(sp):
            def load_block(b, w, row0, col0):
                for s in range(US):
                    if not (isinstance(b, int) and b == 0 and s < SLOTS):
                        sp.wait_ge(lo_ready, US * b + s - SLOTS + 1)
                    src = w[bass.ds(row0 + s * UK * P, UK * P), bass.ds(col0, COLS)]
                    sp.dma_start(raw[s % SLOTS][:, :, :], src.rearrange("(k p) n -> p k n", p=P)) \
                        .then_inc(raw_in[s % SLOTS], 16)

            load_block(B_QKV, w_in, 0, Q0)
            load_block(B_QKV + 1, w_in, 0, K0)
            load_block(B_QKV + 2, w_in, 0, V0)
            with sp.Fori(1, 4) as g:
                load_block(B_QKV + 3 * g, w_in, 0, Q0 + g * COLS)
                load_block(B_QKV + 3 * g + 1, w_in, 0, K0 + g * COLS)
                load_block(B_QKV + 3 * g + 2, w_in, 0, V0 + g * COLS)
            with sp.Fori(0, 4) as m:
                load_block(B_CONV + m, w_in, 0, XBC0 + INNER + m * COLS)
            with sp.Fori(0, 8) as m:
                load_block(B_CONV + 4 + m, w_in, 0, XBC0 + m * COLS)
            with sp.Fori(1, 5) as j1:
                load_block(B_SSD + 4 * j1 - 4, w_in, 0, Z0 + 2 * j1 * COLS - 2 * COLS)
                load_block(B_SSD + 4 * j1 - 3, w_in, 0, GATE0 + j1 * COLS - COLS)
                load_block(B_SSD + 4 * j1 - 2, w_in, 0, Z0 + 2 * j1 * COLS - COLS)
                load_block(B_SSD + 4 * j1 - 1, w_attn_out, 0, j1 * COLS - COLS)
            with sp.Fori(0, 4) as j:
                load_block(B_GATE + j, w_in, 0, GATE0 + D + j * COLS)
            with sp.Fori(0, 4) as j:
                load_block(B_SSM + 2 * j, w_ssm_out, 0, j * COLS)
                load_block(B_SSM + 2 * j + 1, w_ssm_out, D, j * COLS)
            with sp.Fori(0, 4) as j:
                load_block(B_OUT + j, w_out, 0, j * COLS)
            with sp.Fori(0, 4) as q:
                with sp.Fori(0, 4) as u:
                    load_block(B_MLP + 8 * q + u, w_up, 0, q * D + u * COLS)
                with sp.Fori(0, 4) as d:
                    load_block(B_MLP + 8 * q + 4 + d, w_down, q * D, d * COLS)
            for d in range(4):
                sp.wait_ge(set_free[d % 2], 41 + d // 2)
                sp.dma_start(out[:, d * COLS:(d + 1) * COLS].rearrange("(t p) n -> p t n", p=P),
                             h[:, :, d * COLS:(d + 1) * COLS]).then_inc(stored, 16)
            sp.wait_ge(stored, 64)

        @block.tensor
        def _(pe):
            mm = nc.tensor.matmul

            def transpose(dst, src):
                return nc.tensor.transpose(dst, src, ident[:, :])

            def stream(b, k, uses, hi, lo, kt0=0, ready=None, after=None):
                if later(uses):
                    pe.wait_ge(set_free[k], uses)
                for s in range(US):
                    if ready:
                        ready(s)
                    pe.wait_ge(hi_ready, US * b + s + 1)
                    pe.wait_ge(lo_ready, US * b + s + 1)
                    sl = s % SLOTS
                    for kk in range(UK):
                        kt = kt0 + s * UK + kk
                        for t in range(NTOK):
                            dst = SETS[k][t][:, :]
                            xh = hi[:, kt, t * P:(t + 1) * P]
                            xl = lo[:, kt, t * P:(t + 1) * P]
                            mm(dst, xh, whi[sl][:, kk, :], start=(s == 0 and kk == 0), stop=False)
                            mm(dst, xh, wlo[sl][:, kk, :], start=False, stop=False)
                            last = mm(dst, xl, whi[sl][:, kk, :], start=False, stop=(s == US - 1 and kk == UK - 1))
                    last.then_inc(unit_used, 1)
                    for f in (after or {}).get(s, ()):
                        f()

            pe.wait_ge(const_ready, 1)
            pe.wait_ge(par_loaded, 16 * 8)
            nc.tensor.transpose(ps[0][:, 0:CW_C], prow[0:CW_C, 0, :], ident[0:CW_C, 0:CW_C])
            for i in range(2):
                last = nc.tensor.transpose(ps[0][:, 128 * (i + 1):128 * (i + 1) + 96], prow[0:96, 1 + i, :],
                                           ident[0:96, 0:96])
            last.then_inc(par_T, 1)
            XB = [6, 7, 4, 5, 2, 3, 6, 7]
            for i in range(8):
                pe.wait_ge(x_loaded[i // 2], 16)
                if i >= 6:
                    pe.wait_ge(xT_lo_done, 2 * (i - 5))
                for kk in range(2):
                    for t in range(NTOK):
                        kt = 2 * i + kk
                        last = transpose(ps[XB[i]][:, kk * T + t * P:kk * T + (t + 1) * P],
                                         x_in[:, t, kt * P:(kt + 1) * P])
                last.then_inc(x_T, 1)

            def at_transpose(n):
                def f():
                    pe.wait_ge(normed, 2 * n + 2)
                    if later(n):
                        pe.wait_ge(probT_ready, n)
                    transpose(ps[7][:, P:2 * P], prob[:, 0:P])
                    transpose(ps[7][:, 2 * P:3 * P], prob[:, P:2 * P])
                    transpose(ps[7][:, 0:P], prob[:, 2 * P:3 * P]).then_inc(p_T, 1)
                return f

            def at_pv(n, hh):
                def f():
                    pe.wait_ge(probT_ready, n + 1)
                    pe.wait_ge(biased, n + 1)
                    mm(ps[6][:, 0:T], v_st[:, 0, hh * HD:(hh + 1) * HD], probT[:, 0:T], start=True, stop=False)
                    mm(ps[6][:, P:T], v_st[:, 1, hh * HD:(hh + 1) * HD], probT[:, T:T + P], start=False,
                       stop=True).then_inc(pv, 1)
                return f

            def attention(n0, w0):
                a = [{} for _ in range(3)]

                def put(step, f):
                    a[step // 8].setdefault(step % 8, []).append(f)
                put(0, w0)
                for hh in range(4):
                    put(6 * hh, at_scores(n0 + hh, hh))
                    put(6 * hh + 2, at_transpose(n0 + hh))
                    put(6 * hh + 4, at_pv(n0 + hh, hh))
                return a

            def at_scores(n, hh):
                def f():
                    if later(n):
                        pe.wait_ge(aT_lo_done, n)
                    mm(ps[6][:, 0:T], qT[:, hh, P:T], kT[:, hh, :], start=True, stop=True)
                    mm(ps[6][:, T:T + P], qT[:, hh, 0:P], kT[:, hh, 0:P], start=True, stop=True).then_inc(scores, 1)
                return f

            def qk_transposes(g):
                def f():
                    for i, (st, (ba, bb)) in enumerate(((q_st, SETS[0]), (k_st, SETS[1]))):
                        pe.wait_ge(qk_normed, 2 * g + i + 1)
                        pe.wait_ge(set_free[i], g + 1)
                        for hh in range(4):
                            for t in range(NTOK):
                                o = (hh % 2) * T + t * P
                                last = transpose((ba, bb)[hh // 2][:, o:o + P], st[:, t, hh * HD:(hh + 1) * HD])
                        last.then_inc(qk_T, 1)
                return f

            def dt_matmuls():
                pe.wait_ge(dtw_hi_done, 1)
                pe.wait_ge(dtw_lo_done, 1)
                for kt in range(KT):
                    for t in range(NTOK):
                        xh = xT_hi[:, kt, t * P:(t + 1) * P]
                        xl = xT_lo[:, kt, t * P:(t + 1) * P]
                        dst = ps[6 + t][:, 0:SNH]
                        mm(dst, xh, dtw_hi[:, kt, :], start=(kt == 0), stop=False)
                        mm(dst, xh, dtw_lo[:, kt, :], start=False, stop=False)
                        last = mm(dst, xl, dtw_hi[:, kt, :], start=False, stop=(kt == KT - 1))
                last.then_inc(dt_mm, 1)

            def decay_matmuls():
                pe.wait_ge(dt_ready, 1)
                mm(ps[6][:, 0:SNH], strict[:, :], la[:, 0, :], start=True, stop=True)
                mm(ps[6][:, SNH:2 * SNH], tri[:, :], la[:, 1, :], start=True, stop=True).then_inc(dec_mm, 1)

            first = {s: (lambda s=s: pe.wait_ge(xT_lo_done, 2 * s + 2)) for s in range(US)}
            pe.wait_ge(par_ready, 1)
            stream(B_QKV, 0, 0, xT_hi, xT_lo, ready=lambda s: first[s]())
            pe.wait_ge(xT_lo_done, KT)
            stream(B_QKV + 1, 1, 0, xT_hi, xT_lo, after={1: [dt_matmuls], 6: [decay_matmuls]})
            stream(B_QKV + 2, 2, 0, xT_hi, xT_lo, after={4: [qk_transposes(0)]})
            pe.wait_ge(dec_exp, 1)
            def qkv_group(g):
                def start_group():
                    pe.wait_ge(qkT_ready, 2 * g)
                    pe.wait_ge(set_free[2], g)
                a = attention(4 * g - 4, start_group)
                a[2].setdefault(4, []).insert(0, qk_transposes(g))
                pe.wait_ge(qkT_ready, 2 * g - 1)
                stream(B_QKV + 3 * g, 0, g, xT_hi, xT_lo, after=a[0])
                pe.wait_ge(qkT_ready, 2 * g)
                stream(B_QKV + 3 * g + 1, 1, g, xT_hi, xT_lo, after=a[1])
                stream(B_QKV + 3 * g + 2, 2, g, xT_hi, xT_lo, after=a[2])

            qkv_group(1)
            with pe.Fori(2, 4) as g:
                qkv_group(g)

            def conv_T(m, i, staged, backs):
                def f():
                    pe.wait_ge(set_free[i], staged)
                    pe.wait_ge(c_silu, m)
                    pe.wait_ge(c_out, backs)
                    for c in range(4):
                        for t in range(NTOK):
                            o = (c % 2) * T + t * P
                            last = transpose(ps[4 + c // 2][:, o:o + P], c_st[i][:, t, c * P:(c + 1) * P])
                    last.then_inc(c_T, 1)
                return f

            def conv_back(m, src, chunks):
                def f():
                    pe.wait_ge(c_silu, m + 1)
                    for t in range(chunks):
                        for c in range(4):
                            last = transpose(ps[4 + t][:, c * P:(c + 1) * P], src[:, c, t * P:(t + 1) * P])
                    last.then_inc(c_back, 1)
                return f

            def start_last():
                pe.wait_ge(qkT_ready, 8)
                pe.wait_ge(set_free[2], 4)
            a = attention(12, start_last)

            def conv_after(m, i, staged, backs, src=None, chunks=2, more=None):
                d = dict(more or {})
                d[1] = d.get(1, []) + [conv_T(m, i, staged, backs)]
                if src is not None:
                    d[6] = d.get(6, []) + [conv_back(m, src, chunks)]
                return d

            pe.wait_ge(set_free[2], 4)
            pe.wait_ge(qkT_ready, 7)
            stream(B_CONV, 0, 4, xT_hi, xT_lo, after=a[0])
            pe.wait_ge(qkT_ready, 8)
            stream(B_CONV + 1, 1, 4, xT_hi, xT_lo, after=conv_after(0, 0, 5, 0, BT[:, 0:4, :], 1, a[1]))
            stream(B_CONV + 2, 0, 5, xT_hi, xT_lo, after=conv_after(1, 1, 5, 1, BT[:, 4:8, :], 1, a[2]))
            stream(B_CONV + 3, 1, 5, xT_hi, xT_lo, after=conv_after(2, 0, 6, 2))
            stream(B_CONV + 4, 0, 6, xT_hi, xT_lo, after=conv_after(3, 1, 6, 2))
            with pe.Fori(0, 3) as i:
                stream(B_CONV + 5 + 2 * i, 1, 6 + i, xT_hi, xT_lo, after=conv_after(4 + 2 * i, 0, 7 + i, 2 + 2 * i, cT))
                stream(B_CONV + 6 + 2 * i, 0, 7 + i, xT_hi, xT_lo, after=conv_after(5 + 2 * i, 1, 7 + i, 3 + 2 * i, cT))
            stream(B_CONV + 11, 1, 9, xT_hi, xT_lo, after=conv_after(10, 0, 10, 8, cT))
            conv_T(11, 1, 10, 9)()
            conv_back(11, cT, 2)()

            def ssd_state(n, c, g):
                def f():
                    pe.wait_ge(xf_ready, n + 1)
                    if c == 0:
                        if later(g):
                            pe.wait_ge(yo_done, g)
                        mm(ps[7][:, :], Btg[:, :], xd[:, :, :].rearrange("p h d -> p (h d)"), start=True,
                           stop=True).then_inc(st_mm, 1)
                    else:
                        pe.wait_ge(prev_ready, g + 1)
                        mm(ps[7][:, :], CTg[:, P:T], prev[:, :], start=True, stop=True).then_inc(off_mm, 1)
                return f

            def ssd_y(n, c, g):
                def f():
                    pe.wait_ge(M_ready, n + 1)
                    for hh in range(HG):
                        last = mm(ps[6][:, hh * SHD:(hh + 1) * SHD], lm[:, hh, :], xf[:, hh, :], start=True,
                                  stop=True)
                    last.then_inc(y_mm, 1)
                return f

            def ssd_after(n, c, g):
                def seg():
                    pe.wait_ge(g_copied, g + 1)
                    if later(n):
                        pe.wait_ge(yd_done, n)
                    mm(ps[6][:, 0:P], BTg[:, c * P:(c + 1) * P], CTg[:, c * P:(c + 1) * P], start=True,
                       stop=True).then_inc(cb_mm, 1)
                    pe.wait_ge(lm_ready, n + 1)
                    for hh in range(HG):
                        last = mm(ps[4 + hh // 4][:, (hh % 4) * P:(hh % 4 + 1) * P], lm[:, hh, :], tri[:, :],
                                  start=True, stop=True)
                        if hh % 4 == 3:
                            last.then_inc(seg_mm, 1)
                return {1: [seg], 2: [ssd_state(n, c, g)], 4: [ssd_y(n, c, g)]}

            pe.wait_ge(c_out, 10)
            pe.wait_ge(aT_lo_done, NH)
            def ssd_blocks(j):
                b = B_SSD + 4 * j
                stream(b, 0, 10 + 2 * j, xT_hi, xT_lo, after=ssd_after(4 * j, 0, 2 * j))
                stream(b + 1, 1, 10 + 2 * j, xT_hi, xT_lo, after=ssd_after(4 * j + 1, 1, 2 * j))
                stream(b + 2, 0, 11 + 2 * j, xT_hi, xT_lo, after=ssd_after(4 * j + 2, 0, 2 * j + 1))
                stream(b + 3, 1, 11 + 2 * j, aT_hi, aT_lo, after=ssd_after(4 * j + 3, 1, 2 * j + 1))

            ssd_blocks(0)
            with pe.Fori(1, 4) as j:
                ssd_blocks(j)

            def y_transposes(G, i, js):
                def f():
                    pe.wait_ge(y_copied, G + 1)
                    for c in range(4):
                        for t in range(NTOK):
                            o = (c % 2) * T + t * P
                            last = transpose(ps[4 + 2 * i + c // 2][:, o:o + P], y_st[i][:, t, c * P:(c + 1) * P])
                    last.then_inc(y_T, 1)
                return f

            with pe.Fori(0, 2) as i:
                for k in range(2):
                    jb = 2 * i + k
                    G = 2 * jb
                    stream(B_GATE + jb, k, 18 + i, xT_hi, xT_lo,
                           after={1: [y_transposes(G, 0, jb)], 5: [y_transposes(G + 1, 1, jb)]})

            def m_transposes(j):
                def f():
                    pe.wait_ge(m_ready, j + 1)
                    if later(j):
                        pe.wait_ge(gT_lo_done, 2 * j)
                    for c in range(4):
                        for t in range(NTOK):
                            o = (c % 2) * T + t * P
                            last = transpose(ps[4 + c // 2][:, o:o + P], m_st[:, t, c * P:(c + 1) * P])
                    last.then_inc(m_T, 1)
                return f

            pe.wait_ge(sT_lo_done, 2 * KT)
            stream(B_SSM, 0, 20, sT_hi, sT_lo)
            stream(B_SSM + 1, 1, 20, sT_hi, sT_lo, kt0=KT)
            def ssm_out(j):
                stream(B_SSM + 2 * j, 0, 20 + j, sT_hi, sT_lo, after={3: [m_transposes(j - 1)]})
                stream(B_SSM + 2 * j + 1, 1, 20 + j, sT_hi, sT_lo, kt0=KT)
            ssm_out(1)
            with pe.Fori(2, 4) as j:
                ssm_out(j)

            def h_transposes(j):
                def f():
                    pe.wait_ge(set_free[j % 2], 25 + j // 2)
                    ba = 6 if j % 2 == 0 else 4
                    if j == 1:
                        pe.wait_ge(gT_lo_done, 8)
                    if j >= 2:
                        pe.wait_ge(hT_lo_done, 4 * (j - 1))
                    for c in range(4):
                        for t in range(NTOK):
                            o = (c % 2) * T + t * P
                            last = transpose(ps[ba + c // 2][:, o:o + P],
                                             h[:, t, j * COLS + c * P:j * COLS + (c + 1) * P])
                    last.then_inc(h_T, 1)
                return f

            def merged_ready(s):
                if s == 0:
                    pe.wait_ge(gT_lo_done, 6)
                if s == 6:
                    pe.wait_ge(gT_lo_done, 8)
            stream(B_OUT, 0, 24, gT_hi, gT_lo, ready=merged_ready, after={2: [m_transposes(3)]})
            for j in range(1, 4):
                stream(B_OUT + j, j % 2, 24 + j // 2, gT_hi, gT_lo, after={2: [h_transposes(j - 1)]})
            h_transposes(3)()
            pe.wait_ge(hT_lo_done, KT)

            def r_transposes(q, u):
                def f():
                    n = 4 * q + u
                    pe.wait_ge(r_ready, n + 1)
                    ba = 4 + 2 * (u % 2)
                    if not (isinstance(n, int) and n < 2):
                        pe.wait_ge(fT_lo_done, 2 * n - 2)
                    for c in range(4):
                        for t in range(NTOK):
                            o = (c % 2) * T + t * P
                            last = transpose(ps[ba + c // 2][:, o:o + P], r_st[:, t, c * P:(c + 1) * P])
                    last.then_inc(r_T, 1)
                return f

            def mlp(q):
                b = B_MLP + 8 * q
                for u in range(4):
                    stream(b + u, u % 2, 26 + 4 * q + u // 2, hT_hi, hT_lo,
                           after={3: [r_transposes(q, u - 1)]} if u else None)

                def ff_ready(s):
                    if s == 0:
                        pe.wait_ge(fT_lo_done, 8 * q + 6)
                    if s == 6:
                        pe.wait_ge(fT_lo_done, 8 * q + 8)
                stream(b + 4, 0, 28 + 4 * q, fT_hi, fT_lo, ready=ff_ready, after={3: [r_transposes(q, 3)]})
                for d in range(1, 4):
                    stream(b + 4 + d, d % 2, 28 + 4 * q + d // 2, fT_hi, fT_lo)

            mlp(0)
            with pe.Fori(1, 4) as q:
                mlp(q)

        @block.scalar
        def _(act):
            A = nc.scalar.activation

            def split(b, s):
                if s >= US:
                    b, s = b + 1, s - US
                act.wait_ge(raw_in[s % SLOTS], 16 * ((US // SLOTS) * b + s // SLOTS + 1))
                if not (isinstance(b, int) and b == 0 and s < SLOTS):
                    act.wait_ge(unit_used, US * b + s - SLOTS + 1)
                A(whi[s % SLOTS][:, :, :], raw[s % SLOTS][:, :, :], ACT.Copy).then_inc(hi_ready, 1)

            def steps(b, work=None, last=False):
                for s in range(US):
                    if not (last and s + LEAD >= US):
                        split(b, s + LEAD)
                    for f in (work or {}).get(s, ()):
                        f()

            def block_done(b):
                act.wait_ge(unit_used, US * b + US)

            for c in range(4):
                act.dma_start(x_in[:, :, c * COLS:(c + 1) * COLS],
                              x[:, c * COLS:(c + 1) * COLS].rearrange("(t p) n -> p t n", p=P)) \
                    .then_inc(x_loaded[c], 16)
                if c == 0:
                    rows = [(mix_norm_w[0], 16, 0, 0), (mlp_norm_w[0], 16, 0, 16), (ssm_norm_w[0], 32, 0, 32),
                            (conv_b[0], 48, 0, 64), (q_norm_w[0], 1, 0, 112), (k_norm_w[0], 1, 0, 113)]
                    for w, n, s, r in rows:
                        act.dma_start(prow[r:r + n, s, :], w.rearrange("(a b) -> a b", b=P)).then_inc(par_loaded, 16)
                    for i in range(2):
                        act.dma_start(prow[0:96, 1 + i, :],
                                      conv_w[0, 2 * i:2 * i + 2, :].rearrange("k (a b) -> (k a) b", b=P)) \
                            .then_inc(par_loaded, 16)
            act.dma_start(dtw[:, :, :], w_in[:, DT0:DT0 + SNH].rearrange("(k p) n -> p k n", p=P)) \
                .then_inc(dtw_loaded, 16)
            for w, dst in ((dt_bias, dbias), (a_log, alog), (d_skip, dskip)):
                act.dma_start(dst[:, :], w[0].partition_broadcast(P)).then_inc(row_loaded, 16)
            act.wait_ge(par_T, 1)
            A(par[:, 0:CW_C], ps[0][:, 0:CW_C], ACT.Copy)
            A(par[:, CW_C:CW_C + 96], ps[0][:, 128:224], ACT.Copy)
            A(par[:, CW_C + 96:NPAR], ps[0][:, 256:352], ACT.Copy).then_inc(par_ready, 1)
            for s in range(LEAD):
                split(0, s)
            act.wait_ge(par_ready, 1)
            XB = [6, 7, 4, 5, 2, 3, 6, 7]
            for i in range(8):
                act.wait_ge(x_T, i + 1)
                for kk in range(2):
                    kt = 2 * i + kk
                    A(xT_hi[:, kt, :], ps[XB[i]][:, kk * T:(kk + 1) * T], ACT.Copy,
                      scale=par[:, MIX_C + kt:MIX_C + kt + 1]).then_inc(xT_hi_done, 1)

            def x_squares():
                for t in range(NTOK):
                    A(xjunk[t][:, :], x_in[:, t, :], ACT.Square, accum_out=xss[:, t:t + 1]).then_inc(xsq_done, 1)

            def dtw_round():
                act.wait_ge(dtw_loaded, 16)
                A(dtw_hi[:, :, :], dtw[:, :, :], ACT.Copy).then_inc(dtw_hi_done, 1)

            def evac_qk(g, i, st):
                def f():
                    block_done(B_QKV + 3 * g + i)
                    if isinstance(g, int) and g == 0:
                        act.wait_ge(rstd1_ready, 1)
                    else:
                        act.wait_ge(qk_T, 2 * g - 1 + i)
                    A(st[:, 0, :], SETS[i][0][:, :], ACT.Copy, scale=rstd1[:, 0:1])
                    A(st[:, 1, :], SETS[i][1][:, :], ACT.Copy, scale=rstd1[:, 1:2]).then_inc(set_free[i], 1)
                return f

            def evac_v(g):
                def f():
                    block_done(B_QKV + 3 * g + 2)
                    if later(g):
                        act.wait_ge(pv, 4 * g)
                    A(v_st[:, 0, :], SETS[2][0][:, :], ACT.Copy, scale=rstd1[:, 0:1])
                    A(v_st[:, 1, :], SETS[2][1][:, :], ACT.Copy, scale=rstd1[:, 1:2]).then_inc(set_free[2], 1)
                return f

            def evac_qkT(g):
                def f():
                    for i, (dst, w) in enumerate(((qT, QN_C), (kT, KN_C))):
                        act.wait_ge(qk_T, 2 * g + i + 1)
                        act.wait_ge(const_ready, 2)
                        if later(g):
                            act.wait_ge(scores, 4 * g)
                        A(dst[:, 0:2, :], heads(SETS[i][0][:, :], 2), ACT.Copy, scale=par[:, w:w + 1])
                        A(dst[:, 2:4, :], heads(SETS[i][1][:, :], 2), ACT.Copy, scale=par[:, w:w + 1]) \
                            .then_inc(qkT_ready, 1)
                return f

            def at_exp(n):
                def f():
                    act.wait_ge(maxed, 2 * n + 2)
                    if later(n):
                        act.wait_ge(normed, 2 * n)
                    A(prob[:, 0:T], prob[:, 0:T], ACT.Exp, bias=negmax[:, 0:1], accum_out=psum_[:, 0:1])
                    A(prob[:, T:T + P], prob[:, T:T + P], ACT.Exp, bias=negmax[:, 1:2],
                      accum_out=psum_[:, 1:2]).then_inc(expd, 1)
                return f

            def at_copy(n):
                def f():
                    act.wait_ge(p_T, n + 1)
                    if later(n):
                        act.wait_ge(pv, n)
                    A(probT[:, :], ps[7][:, 0:3 * P], ACT.Copy).then_inc(probT_ready, 1)
                return f

            def at_hi(n):
                def f():
                    act.wait_ge(pv, n + 1)
                    A(aT_hi[:, bass.ds(n, 1), :].rearrange("p a t -> p (a t)"), ps[6][:, 0:T], ACT.Copy) \
                        .then_inc(aT_hi_done, 1)
                return f

            def attention(n0):
                a = [{} for _ in range(3)]

                def put(step, f):
                    a[step // 8].setdefault(step % 8, []).append(f)
                for hh in range(4):
                    put(6 * hh + 1, at_exp(n0 + hh))
                    put(6 * hh + 2, at_copy(n0 + hh))
                    put(6 * hh + 4, at_hi(n0 + hh))
                return a

            def dt_chain():
                act.wait_ge(dt_mm, 1)
                for t in range(NTOK):
                    i = A(dts[0][:, t, :], ps[6 + t][:, 0:SNH], ACT.Copy, scale=rstd1[:, t:t + 1])
                i.then_inc(dt_s, 1)
                act.wait_ge(dt_v, 3)
                A(dts[3][:, :, :], dts[2][:, :, :], ACT.Exp).then_inc(dt_s, 1)
                act.wait_ge(dt_v, 4)
                A(dts[5][:, :, :], dts[4][:, :, :], ACT.Ln).then_inc(dt_s, 1)
                act.wait_ge(row_loaded, 48)
                A(alog[:, :], alog[:, :], ACT.Exp).then_inc(dt_s, 1)

            def dec_chain():
                act.wait_ge(dec_mm, 1)
                A(dtd[:, :], ps[6][:, 0:SNH], ACT.Exp)
                A(eac[:, :], ps[6][:, SNH:2 * SNH], ACT.Exp).then_inc(dec_exp, 1)

            def add(d, step, f):
                d.setdefault(step, []).append(f)
                return d

            steps(B_QKV, {0: [dtw_round], 1: [x_squares], 7: [evac_qk(0, 0, q_st)]})
            steps(B_QKV + 1, {1: [dt_chain], 6: [dec_chain], 7: [evac_qk(0, 1, k_st)]})
            steps(B_QKV + 2, {4: [evac_qkT(0)], 7: [evac_v(0)]})
            def qkv_group(g):
                a = attention(4 * g - 4)
                steps(B_QKV + 3 * g, add(a[0], 7, evac_qk(g, 0, q_st)))
                steps(B_QKV + 3 * g + 1, add(a[1], 7, evac_qk(g, 1, k_st)))
                a[2].setdefault(4, []).insert(0, evac_qkT(g))
                steps(B_QKV + 3 * g + 2, add(a[2], 7, evac_v(g)))

            qkv_group(1)
            with act.Fori(2, 4) as g:
                qkv_group(g)

            def conv_evac(m, k, i):
                def f():
                    block_done(B_CONV + m)
                    if not (isinstance(m, int) and m < 2):
                        act.wait_ge(c_T, m - 1)
                    A(c_st[i][:, 0, :], SETS[k][0][:, :], ACT.Copy, scale=rstd1[:, 0:1])
                    A(c_st[i][:, 1, :], SETS[k][1][:, :], ACT.Copy, scale=rstd1[:, 1:2]).then_inc(set_free[k], 1)
                return f

            def conv_first(m):
                def f():
                    act.wait_ge(c_T, m + 1)
                    act.wait_ge(c_par, m + 1)
                    if later(m):
                        act.wait_ge(c_silu, m)
                    for c in range(4):
                        i = A(cacc[:, c, :], ps[4 + c // 2][:, (c % 2) * T:(c % 2 + 1) * T], ACT.Identity,
                              scale=cw[:, 3, c:c + 1], bias=cb[:, c:c + 1])
                        if c % 2:
                            i.then_inc(c_first, 1)
                return f

            def conv_silu(m, dst):
                def f():
                    act.wait_ge(c_tap, 12 * m + 12)
                    A(dst, cacc[:, :, :], ACT.Silu).then_inc(c_silu, 1)
                return f

            def conv_out(m, kind):
                def f():
                    if kind != "C":
                        act.wait_ge(c_back, back_count(m))
                    if kind == "B":
                        A(Btok[:, m * COLS:(m + 1) * COLS], ps[4][:, :], ACT.Copy).then_inc(c_out, 1)
                    if kind == "x":
                        g = m - 4
                        A(xs[:, bass.ds(g, 1), 0, :].rearrange("p a n -> p (a n)"), ps[4][:, :], ACT.Copy)
                        A(xs[:, bass.ds(g, 1), 1, :].rearrange("p a n -> p (a n)"), ps[5][:, :], ACT.Copy) \
                            .then_inc(c_out, 1)
                return f

            def back_count(m):
                return m + 1 if isinstance(m, int) and m < 2 else m - 1

            def conv_work(m, dst, kind, evac_f, more=None):
                d = dict(more or {})
                add(d, 1, conv_first(m))
                add(d, 4, conv_silu(m, dst))
                if kind != "C":
                    add(d, 6, conv_out(m, kind))
                if evac_f:
                    add(d, 7, evac_f)
                return d

            a = attention(12)
            steps(B_CONV, add(a[0], 7, conv_evac(0, 0, 0)))
            steps(B_CONV + 1, conv_work(0, BT[:, 0:4, :], "B", conv_evac(1, 1, 1), a[1]))
            steps(B_CONV + 2, conv_work(1, BT[:, 4:8, :], "B", conv_evac(2, 0, 0), a[2]))
            steps(B_CONV + 3, conv_work(2, CT[:, 0:4, :], "C", conv_evac(3, 1, 1)))
            steps(B_CONV + 4, conv_work(3, CT[:, 4:8, :], "C", conv_evac(4, 0, 0)))
            with act.Fori(0, 3) as i:
                steps(B_CONV + 5 + 2 * i, conv_work(4 + 2 * i, cT[:, :, :], "x", conv_evac(5 + 2 * i, 1, 1)))
                steps(B_CONV + 6 + 2 * i, conv_work(5 + 2 * i, cT[:, :, :], "x", conv_evac(6 + 2 * i, 0, 0)))
            steps(B_CONV + 11, conv_work(10, cT[:, :, :], "x", conv_evac(11, 1, 1)))
            conv_first(11)()
            conv_silu(11, cT[:, :, :])()
            conv_out(11, "x")()

            def ssd_exp(n):
                def f():
                    for i in range(2):
                        act.wait_ge(seg_mm, 2 * n + i + 1)
                        A(lm[:, 4 * i:4 * i + 4, :], heads(ps[4 + i][:, :], 4), ACT.Exp).then_inc(dec_done, 1)
                return f

            def ssd_prev(g):
                def f():
                    act.wait_ge(st_mm, g + 1)
                    if later(g):
                        act.wait_ge(off_mm, g)
                    A(prev[:, :], ps[7][:, :], ACT.Copy).then_inc(prev_ready, 1)
                return f

            def z_sigmoid(b, g):
                def f():
                    block_done(b)
                    if later(g):
                        act.wait_ge(yz_done, g)
                        act.wait_ge(ysq_done, 2 * g)
                    for t in range(NTOK):
                        A(zs[:, t, :], SETS[0][t][:, :], ACT.Sigmoid, scale=rstd1[:, t:t + 1]).then_inc(z_sig, 1)
                return f

            def agate(b, j):
                def f():
                    block_done(b)
                    for t in range(NTOK):
                        i = A(merged[:, t, bass.ds(j * COLS, COLS)], SETS[1][t][:, :], ACT.Sigmoid,
                              scale=rstd1[:, t:t + 1])
                    i.then_inc(set_free[1], 1)
                return f

            def y_squares(g):
                def f():
                    act.wait_ge(yz_done, g + 1)
                    if later(g):
                        act.wait_ge(yrs_done, g)
                    for t in range(NTOK):
                        A(zs[:, t, :], xs[:, bass.ds(g, 1), t, :].rearrange("p a n -> p (a n)"), ACT.Square,
                          accum_out=gss[:, t:t + 1]).then_inc(ysq_done, 1)
                return f

            def ssd_blocks(j):
                b = B_SSD + 4 * j
                n = 4 * j
                g = 2 * j
                steps(b, {2: [ssd_exp(n)], 3: [ssd_prev(g)], 7: [z_sigmoid(b, g)]})
                steps(b + 1, {2: [ssd_exp(n + 1)], 6: [y_squares(g)], 7: [agate(b + 1, j)]})
                steps(b + 2, {2: [ssd_exp(n + 2)], 3: [ssd_prev(g + 1)], 7: [z_sigmoid(b + 2, g + 1)]})
                steps(b + 3, {2: [ssd_exp(n + 3)], 6: [y_squares(g + 1)]})

            ssd_blocks(0)
            with act.Fori(1, 4) as j:
                ssd_blocks(j)

            def sgate_evac(b, k, j):
                def f():
                    block_done(b)
                    for t in range(NTOK):
                        i = A(sgate[:, t, bass.ds(j * COLS, COLS)], SETS[k][t][:, :], ACT.Sigmoid,
                              scale=rstd1[:, t:t + 1])
                    i.then_inc(set_free[k], 1)
                return f

            def s_hi(G, i):
                def f():
                    act.wait_ge(y_T, G + 1)
                    for c in range(4):
                        A(sT_hi[:, bass.ds(4 * G + c, 1), :].rearrange("p a t -> p (a t)"),
                          ps[4 + 2 * i + c // 2][:, (c % 2) * T:(c % 2 + 1) * T], ACT.Copy,
                          scale=sw[i][:, c:c + 1]).then_inc(sT_hi_done, 1)
                return f

            with act.Fori(0, 2) as i:
                for k in range(2):
                    jb = 2 * i + k
                    steps(B_GATE + jb, {1: [s_hi(2 * jb, 0)], 5: [s_hi(2 * jb + 1, 1)],
                                        7: [sgate_evac(B_GATE + jb, k, jb)]})

            def half_evac(j):
                def f():
                    block_done(B_SSM + 2 * j)
                    if later(j):
                        act.wait_ge(m_step, 3 * j)
                    for t in range(NTOK):
                        i = A(s_half[:, t, :], SETS[0][t][:, :], ACT.Copy)
                    i.then_inc(set_free[0], 1)
                return f

            def g_hi(j):
                def f():
                    act.wait_ge(m_T, j + 1)
                    for i in range(2):
                        A(gT_hi[:, bass.ds(4 * j + 2 * i, 2), :], heads(ps[4 + i][:, :], 2), ACT.Copy) \
                            .then_inc(gT_hi_done, 1)
                return f

            steps(B_SSM, {7: [half_evac(0)]})
            steps(B_SSM + 1)
            with act.Fori(1, 4) as j:
                steps(B_SSM + 2 * j, {3: [g_hi(j - 1)], 7: [half_evac(j)]})
                steps(B_SSM + 2 * j + 1)

            def reload_x():
                act.wait_ge(m_ready, 4)
                act.dma_start(h[:, :, :], x.rearrange("(t p) n -> p t n", p=P)).then_inc(x_again, 16)

            def h_squares(j):
                def f():
                    act.wait_ge(set_free[j % 2], 25 + j // 2)
                    act.wait_ge(h_sq, 2 * j)
                    for t in range(NTOK):
                        A(zs[:, t, :], h[:, t, j * COLS:(j + 1) * COLS], ACT.Square,
                          accum_out=hss[:, t, j:j + 1]).then_inc(h_sq, 1)
                return f

            def h_hi(j):
                def f():
                    act.wait_ge(h_T, j + 1)
                    ba = 6 if j % 2 == 0 else 4
                    for c in range(4):
                        kt = 4 * j + c
                        A(hT_hi[:, kt, :], ps[ba + c // 2][:, (c % 2) * T:(c % 2 + 1) * T], ACT.Copy,
                          scale=par[:, MLP_C + kt:MLP_C + kt + 1]).then_inc(hT_hi_done, 1)
                return f

            steps(B_OUT, {2: [g_hi(3), reload_x]})
            for j in range(1, 4):
                steps(B_OUT + j, {1: [h_squares(j - 1)], 2: [h_hi(j - 1)]})
            h_hi(3)()
            h_squares(3)()

            def relu(b, k, n):
                def f():
                    block_done(b)
                    if later(n):
                        act.wait_ge(r_T, n)
                    for t in range(NTOK):
                        i = A(r_st[:, t, :], SETS[k][t][:, :], ACT.Relu, scale=rstd2[:, t:t + 1])
                    i.then_inc(set_free[k], 1)
                return f

            def f_hi(n, u):
                def f():
                    act.wait_ge(r_T, n + 1)
                    for i in range(2):
                        A(fT_hi[:, 4 * u + 2 * i:4 * u + 2 * i + 2, :], heads(ps[4 + 2 * (u % 2) + i][:, :], 2),
                          ACT.Copy).then_inc(fT_hi_done, 1)
                return f

            act.wait_ge(rstd2_ready, 1)

            def mlp(q, end=False):
                b = B_MLP + 8 * q
                for u in range(4):
                    w = {7: [relu(b + u, u % 2, 4 * q + u)]}
                    if u:
                        w[3] = [f_hi(4 * q + u - 1, u - 1)]
                    steps(b + u, w)
                steps(b + 4, {3: [f_hi(4 * q + 3, 3)]})
                for d in range(1, 4):
                    steps(b + 4 + d, last=end and d == 3)

            mlp(0)
            with act.Fori(1, 3) as q:
                mlp(q)
            mlp(3, end=True)

        @block.vector
        def _(dve):
            V = nc.vector

            def split(b, s):
                if s >= US:
                    b, s = b + 1, s - US
                dve.wait_ge(hi_ready, US * b + s + 1)
                V.tensor_tensor(wlo[s % SLOTS][:, :, :], raw[s % SLOTS][:, :, :], fp(whi[s % SLOTS][:, :, :]),
                                ALU.subtract).then_inc(lo_ready, 1)

            def steps(b, work=None, last=False):
                for s in range(US):
                    if not (last and s + LEAD >= US):
                        split(b, s + LEAD)
                    for f in (work or {}).get(s, ()):
                        f()

            def block_done(b):
                dve.wait_ge(unit_used, US * b + US)

            for s in range(LEAD):
                split(0, s)
            dve.wait_ge(par_ready, 1)
            XB = [6, 7, 4, 5, 2, 3, 6, 7]
            for i in range(8):
                dve.wait_ge(xT_hi_done, 2 * i + 2)
                for kk in range(2):
                    kt = 2 * i + kk
                    V.scalar_tensor_tensor(xT_lo[:, kt, :], ps[XB[i]][:, kk * T:(kk + 1) * T],
                                           par[:, MIX_C + kt:MIX_C + kt + 1], fp(xT_hi[:, kt, :]), ALU.mult,
                                           ALU.subtract).then_inc(xT_lo_done, 1)

            def dtw_rest():
                dve.wait_ge(dtw_hi_done, 1)
                V.tensor_tensor(dtw_lo[:, :, :], dtw[:, :, :], fp(dtw_hi[:, :, :]), ALU.subtract) \
                    .then_inc(dtw_lo_done, 1)

            def x_mean():
                dve.wait_ge(xsq_done, 2)
                V.tensor_scalar(xss[:, :], xss[:, :], 1.0 / D, EPS, ALU.mult, ALU.add).then_inc(xms_done, 1)

            dtc = [0]

            def link(ins):
                dtc[0] += 1
                ins.then_inc(dt_v, 1)
                return dtc[0]

            def dt_chain():
                X, NG, NX, E_, W_, L_, R_, S_ = (t[:, :, :] for t in dts)
                dve.wait_ge(dt_s, 1)
                dve.wait_ge(row_loaded, 48)
                link(V.tensor_tensor(X, X, over(dbias[:, :], 1, NTOK), ALU.add))
                dve.wait_ge(dt_v, 1)
                link(V.tensor_scalar(NG, X, -1.0, None, ALU.mult))
                dve.wait_ge(dt_v, 2)
                link(V.tensor_tensor(NX, X, NG, ALU.min))
                dve.wait_ge(dt_s, 2)
                link(V.tensor_scalar(W_, E_, 1.0, None, ALU.add))
                dve.wait_ge(dt_v, 4)
                link(V.tensor_scalar(R_, W_, -1.0, None, ALU.add))
                dve.wait_ge(dt_v, 5)
                link(V.scalar_tensor_tensor(S_, R_, 0.0, E_, ALU.is_equal, ALU.mult))
                link(V.tensor_scalar(NG, R_, 2.0 ** -24, None, ALU.max))
                dve.wait_ge(dt_v, 7)
                link(V.reciprocal(R_, NG))
                dve.wait_ge(dt_s, 3)
                link(V.tensor_tensor(L_, L_, E_, ALU.mult))
                dve.wait_ge(dt_v, 9)
                link(V.tensor_tensor(L_, L_, R_, ALU.mult))
                dve.wait_ge(dt_v, 10)
                link(V.tensor_tensor(L_, L_, S_, ALU.add))
                dve.wait_ge(dt_v, 11)
                link(V.scalar_tensor_tensor(dt_[:, :, :], X, 0.0, L_, ALU.max, ALU.add))
                dve.wait_ge(dt_v, 12)
                dve.wait_ge(dt_s, 4)
                V.scalar_tensor_tensor(la[:, :, :], dt_[:, :, :], -1.0, over(alog[:, :], 1, NTOK), ALU.mult,
                                       ALU.mult).then_inc(dt_ready, 1)

            def dec_chain():
                dve.wait_ge(dec_exp, 1)
                V.tensor_tensor(dtd[:, :], dtd[:, :], dt_[:, 0, :], ALU.mult).then_inc(dt_ready, 1)

            def qk_sums(g, i):
                def f():
                    n = 2 * g + i
                    dve.wait_ge(qk_sq, n + 1)
                    if later(n):
                        dve.wait_ge(qk_rstd, n)
                    V.tensor_reduce(ssum[:, :], sq[:, :, :], AX.X, ALU.add).then_inc(qk_sum, 1)
                    dve.wait_ge(qk_sum, n + 1)
                    V.tensor_scalar(ssum[:, :], ssum[:, :], 1.0 / HD, EPS, ALU.mult, ALU.add).then_inc(qk_ms, 1)
                return f

            def qk_norm(g, i, st):
                def f():
                    n = 2 * g + i
                    dve.wait_ge(qk_rstd, n + 1)
                    v = st[:, :, :].rearrange("p t (h d) -> p (t h) d", d=HD)
                    V.tensor_tensor(v, v, over(rqk[:, :], 2, HD), ALU.mult).then_inc(qk_normed, 1)
                return f

            def at_bias(n, hh):
                def f():
                    dve.wait_ge(scores, n + 1)
                    if hh == 0:
                        dve.wait_ge(slope_done, (n // 4 if isinstance(n, int) else slope_group[0]) + 1)
                    if later(n):
                        dve.wait_ge(p_T, n)
                    V.scalar_tensor_tensor(prob[:, :], dist[:, :], negslope[:, hh:hh + 1], ps[6][:, 0:3 * P],
                                           ALU.mult, ALU.add).then_inc(biased, 1)
                    dve.wait_ge(biased, n + 1)
                    V.tensor_reduce(negmax[:, 0:1], prob[:, 0:T], AX.X, ALU.max, negate=True).then_inc(maxed, 1)
                    V.tensor_reduce(negmax[:, 1:2], prob[:, T:T + P], AX.X, ALU.max, negate=True) \
                        .then_inc(maxed, 1)
                    if hh == 3:
                        V.tensor_scalar(negslope[:, :], negslope[:, :], 0.25, None, ALU.mult) \
                            .then_inc(slope_done, 1)
                return f
            slope_group = [0]

            def at_norm(n):
                def f():
                    dve.wait_ge(expd, n + 1)
                    V.reciprocal(pinv[:, :], psum_[:, :]).then_inc(inv_done, 1)
                    dve.wait_ge(inv_done, n + 1)
                    V.tensor_scalar(prob[:, 0:T], prob[:, 0:T], pinv[:, 0:1], None, ALU.mult).then_inc(normed, 1)
                    V.tensor_scalar(prob[:, T:T + P], prob[:, T:T + P], pinv[:, 1:2], None, ALU.mult) \
                        .then_inc(normed, 1)
                return f

            def at_lo(n):
                def f():
                    dve.wait_ge(aT_hi_done, n + 1)
                    V.tensor_tensor(aT_lo[:, bass.ds(n, 1), :].rearrange("p a t -> p (a t)"), ps[6][:, 0:T],
                                    fp(aT_hi[:, bass.ds(n, 1), :].rearrange("p a t -> p (a t)")),
                                    ALU.subtract).then_inc(aT_lo_done, 1)
                return f

            def attention(n0, g):
                a = [{} for _ in range(3)]
                slope_group[0] = g

                def put(step, f):
                    a[step // 8].setdefault(step % 8, []).append(f)
                for hh in range(4):
                    put(6 * hh, at_bias(n0 + hh, hh))
                    put(6 * hh + 1, at_norm(n0 + hh))
                    put(6 * hh + 4, at_lo(n0 + hh))
                return a

            def add(d, step, f):
                d.setdefault(step, []).append(f)
                return d

            steps(B_QKV, {0: [dtw_rest], 2: [x_mean]})
            steps(B_QKV + 1, {1: [dt_chain, qk_sums(0, 0)], 3: [qk_norm(0, 0, q_st)], 6: [dec_chain]})
            steps(B_QKV + 2, {1: [qk_sums(0, 1)], 3: [qk_norm(0, 1, k_st)]})
            def qkv_group(g):
                a = attention(4 * g - 4, g - 1)
                add(a[1], 1, qk_sums(g, 0))
                add(a[1], 3, qk_norm(g, 0, q_st))
                add(a[2], 1, qk_sums(g, 1))
                add(a[2], 3, qk_norm(g, 1, k_st))
                for i in range(3):
                    steps(B_QKV + 3 * g + i, a[i])

            qkv_group(1)
            with dve.Fori(2, 4) as g:
                qkv_group(g)

            def conv_taps(m, half, tap):
                def f():
                    n0 = 12 * m + 6 * half
                    if tap == 0:
                        dve.wait_ge(c_first, 2 * m + half + 1)
                    for tp in ([0], [1, 2])[tap]:
                        for cc in range(2):
                            c = 2 * half + cc
                            sh = tp + 1
                            if tp:
                                dve.wait_ge(c_tap, n0 + 2 * tp - 1 + cc)
                            V.scalar_tensor_tensor(cacc[:, c, sh:T], ps[4 + half][:, cc * T:cc * T + T - sh],
                                                   cw[:, 2 - tp, c:c + 1], cacc[:, c, sh:T], ALU.mult,
                                                   ALU.add).then_inc(c_tap, 1)
                return f

            def conv_work(m, more=None):
                d = dict(more or {})
                add(d, 1, conv_taps(m, 0, 0))
                add(d, 2, conv_taps(m, 0, 1))
                add(d, 3, conv_taps(m, 1, 0))
                add(d, 3, conv_taps(m, 1, 1))
                return d

            a = attention(12, 3)
            steps(B_CONV, a[0])
            steps(B_CONV + 1, conv_work(0, a[1]))
            steps(B_CONV + 2, conv_work(1, a[2]))
            steps(B_CONV + 3, conv_work(2))
            steps(B_CONV + 4, conv_work(3))
            with dve.Fori(0, 3) as i:
                steps(B_CONV + 5 + 2 * i, conv_work(4 + 2 * i))
                steps(B_CONV + 6 + 2 * i, conv_work(5 + 2 * i))
            steps(B_CONV + 11, conv_work(10))
            for half in range(2):
                for tap in range(2):
                    conv_taps(11, half, tap)()

            def xs_at(g, t):
                return xs[:, bass.ds(g, 1), t, :].rearrange("p a n -> p (a n)")

            def ssd_cbm(n):
                def f():
                    dve.wait_ge(cb_mm, n + 1)
                    V.tensor_tensor(cbm[:, :], ps[6][:, 0:P], tri[:, :], ALU.mult).then_inc(cbm_done, 1)
                return f

            def ssd_M(n):
                def f():
                    dve.wait_ge(cbm_done, n + 1)
                    dve.wait_ge(dec_done, 2 * n + 2)
                    V.tensor_tensor(lm[:, :, :], lm[:, :, :], over(cbm[:, :], 1, HG), ALU.mult) \
                        .then_inc(M_ready, 1)
                return f

            def ssd_y(n, c, g):
                def f():
                    dve.wait_ge(y_mm, n + 1)
                    dve.wait_ge(skip_ready, n + 1)
                    V.tensor_tensor(xs_at(g, c), xs_at(g, c), ps[6][:, :], ALU.add).then_inc(yd_done, 1)
                    if c == 1:
                        dve.wait_ge(off_mm, g + 1)
                        V.tensor_tensor(yoff[:, :, :], heads(ps[7][:, :], HG),
                                        over(eac[:, bass.ds(g * HG, HG)], 2, SHD), ALU.mult).then_inc(yo_done, 1)
                        dve.wait_ge(yo_done, g + 1)
                        dve.wait_ge(yd_done, n + 1)
                        V.tensor_tensor(xs_at(g, c), xs_at(g, c), yoff[:, :, :].rearrange("p h d -> p (h d)"),
                                        ALU.add).then_inc(y_done, 1)
                return f

            def z_gate(g):
                def f():
                    for t in range(NTOK):
                        dve.wait_ge(z_sig, 2 * g + 2)
                        i = V.scalar_tensor_tensor(zs[:, t, :], SETS[0][t][:, :], rstd1[:, t:t + 1], zs[:, t, :],
                                                   ALU.mult, ALU.mult)
                    i.then_inc(set_free[0], 1)
                return f

            def y_gated(g, k):
                def f():
                    dve.wait_ge(y_done, g + 1)
                    dve.wait_ge(set_free[0], 11 + g)
                    v = xs[:, bass.ds(g, 1), :, :].rearrange("p a t n -> p (a t) n")
                    V.tensor_tensor(v, v, zs[:, :, :], ALU.mult).then_inc(yz_done, 1)
                return f

            def y_norm(g):
                def f():
                    dve.wait_ge(ysq_done, 2 * g + 2)
                    if later(g):
                        dve.wait_ge(yrs_done, g)
                    V.tensor_scalar(gss[:, :], gss[:, :], 1.0 / GW, EPS, ALU.mult, ALU.add).then_inc(yms_done, 1)
                    dve.wait_ge(yrs_done, g + 1)
                    for t in range(NTOK):
                        V.tensor_scalar(xs_at(g, t), xs_at(g, t), grs[:, t:t + 1], None, ALU.mult) \
                            .then_inc(yfin, 1)
                return f

            def merge_attn(b, j):
                def f():
                    block_done(b)
                    dve.wait_ge(set_free[1], 11 + 2 * j)
                    for t in range(NTOK):
                        v = merged[:, t, bass.ds(j * COLS, COLS)]
                        i = V.tensor_tensor(v, v, SETS[1][t][:, :], ALU.mult)
                    i.then_inc(set_free[1], 1)
                return f

            def ssd_blocks(j):
                b = B_SSD + 4 * j
                n = 4 * j
                g = 2 * j
                steps(b, {1: [ssd_cbm(n)], 3: [ssd_M(n)], 5: [ssd_y(n, 0, g)], 7: [z_gate(g)]})
                steps(b + 1, {1: [ssd_cbm(n + 1)], 3: [ssd_M(n + 1)], 5: [ssd_y(n + 1, 1, g)],
                              6: [y_gated(g, 0)], 7: [y_norm(g)]})
                steps(b + 2, {1: [ssd_cbm(n + 2)], 3: [ssd_M(n + 2)], 5: [ssd_y(n + 2, 0, g + 1)],
                              7: [z_gate(g + 1)]})
                steps(b + 3, {1: [ssd_cbm(n + 3)], 3: [ssd_M(n + 3)], 5: [ssd_y(n + 3, 1, g + 1)],
                              6: [y_gated(g + 1, 1)], 7: [y_norm(g + 1), merge_attn(b + 3, j)]})

            ssd_blocks(0)
            with dve.Fori(1, 4) as j:
                ssd_blocks(j)

            def s_lo(G, i):
                def f():
                    for half in range(2):
                        dve.wait_ge(sT_hi_done, 4 * G + 2 * half + 2)
                        for cc in range(2):
                            c = 2 * half + cc
                            V.scalar_tensor_tensor(
                                sT_lo[:, bass.ds(4 * G + c, 1), :].rearrange("p a t -> p (a t)"),
                                ps[4 + 2 * i + half][:, cc * T:(cc + 1) * T], sw[i][:, c:c + 1],
                                fp(sT_hi[:, bass.ds(4 * G + c, 1), :].rearrange("p a t -> p (a t)")),
                                ALU.mult, ALU.subtract).then_inc(sT_lo_done, 1)
                return f

            with dve.Fori(0, 4) as jb:
                steps(B_GATE + jb, {1: [s_lo(2 * jb, 0)], 5: [s_lo(2 * jb + 1, 1)]})

            def merge_ssm(j):
                def f():
                    block_done(B_SSM + 2 * j + 1)
                    dve.wait_ge(set_free[0], 21 + j)
                    if later(j):
                        dve.wait_ge(m_T, j)
                    for t in range(NTOK):
                        V.tensor_tensor(m_st[:, t, :], SETS[1][t][:, :], s_half[:, t, :], ALU.add) \
                            .then_inc((m_step, set_free[1])[t], 1)
                    for t in range(NTOK):
                        dve.wait_ge((m_step, set_free[1])[t], (3 * j + 1, 21 + j)[t])
                        V.tensor_tensor(m_st[:, t, :], m_st[:, t, :], sgate[:, t, bass.ds(j * COLS, COLS)],
                                        ALU.mult).then_inc(m_step, 1)
                return f

            def g_lo(j):
                def f():
                    for i in range(2):
                        dve.wait_ge(gT_hi_done, 2 * j + i + 1)
                        V.tensor_tensor(gT_lo[:, bass.ds(4 * j + 2 * i, 2), :], heads(ps[4 + i][:, :], 2),
                                        fp(gT_hi[:, bass.ds(4 * j + 2 * i, 2), :]), ALU.subtract) \
                            .then_inc(gT_lo_done, 1)
                return f

            steps(B_SSM)
            steps(B_SSM + 1, {7: [merge_ssm(0)]})
            with dve.Fori(1, 4) as j:
                steps(B_SSM + 2 * j, {3: [g_lo(j - 1)]})
                steps(B_SSM + 2 * j + 1, {7: [merge_ssm(j)]})

            def h_add(j):
                def f():
                    block_done(B_OUT + j)
                    dve.wait_ge(x_again, 16)
                    for t in range(NTOK):
                        v = h[:, t, j * COLS:(j + 1) * COLS]
                        i = V.tensor_tensor(v, v, SETS[j % 2][t][:, :], ALU.add)
                    i.then_inc(set_free[j % 2], 1)
                return f

            def h_lo(j):
                def f():
                    ba = 6 if j % 2 == 0 else 4
                    for half in range(2):
                        dve.wait_ge(hT_hi_done, 4 * j + 2 * half + 2)
                        for cc in range(2):
                            kt = 4 * j + 2 * half + cc
                            V.scalar_tensor_tensor(hT_lo[:, kt, :], ps[ba + half][:, cc * T:(cc + 1) * T],
                                                   par[:, MLP_C + kt:MLP_C + kt + 1], fp(hT_hi[:, kt, :]),
                                                   ALU.mult, ALU.subtract).then_inc(hT_lo_done, 1)
                return f

            steps(B_OUT, {2: [g_lo(3)], 7: [h_add(0)]})
            for j in range(1, 4):
                steps(B_OUT + j, {2: [h_lo(j - 1)], 7: [h_add(j)]})
            h_lo(3)()
            dve.wait_ge(h_sq, 8)
            V.tensor_reduce(hs2[:, :], hss[:, :, :], AX.X, ALU.add).then_inc(hsum_done, 1)
            dve.wait_ge(hsum_done, 1)
            V.tensor_scalar(hs2[:, :], hs2[:, :], 1.0 / D, EPS, ALU.mult, ALU.add).then_inc(hms_done, 1)

            def f_lo(n, u):
                def f():
                    for i in range(2):
                        dve.wait_ge(fT_hi_done, 2 * n + i + 1)
                        V.tensor_tensor(fT_lo[:, 4 * u + 2 * i:4 * u + 2 * i + 2, :],
                                        heads(ps[4 + 2 * (u % 2) + i][:, :], 2),
                                        fp(fT_hi[:, 4 * u + 2 * i:4 * u + 2 * i + 2, :]), ALU.subtract) \
                            .then_inc(fT_lo_done, 1)
                return f

            def h_down(q, d):
                def f():
                    block_done(B_MLP + 8 * q + 4 + d)
                    for t in range(NTOK):
                        v = h[:, t, d * COLS:(d + 1) * COLS]
                        i = V.tensor_tensor(v, v, SETS[d % 2][t][:, :], ALU.add)
                    i.then_inc(set_free[d % 2], 1)
                return f

            def mlp(q, end=False):
                b = B_MLP + 8 * q
                for u in range(4):
                    steps(b + u, {3: [f_lo(4 * q + u - 1, u - 1)]} if u else None)
                steps(b + 4, {3: [f_lo(4 * q + 3, 3)], 7: [h_down(q, 0)]})
                for d in range(1, 4):
                    steps(b + 4 + d, {7: [h_down(q, d)]}, last=end and d == 3)

            with dve.Fori(0, 3) as q:
                mlp(q)
            mlp(3, end=True)

        @block.gpsimd
        def _(pool):
            G = nc.gpsimd
            G.memset(ident[:, :], 0.0).then_inc(const_step, 1)
            G.memset(tri[:, :], 1.0).then_inc(const_step, 1)
            G.memset(strict[:, :], 1.0).then_inc(const_step, 1)
            pool.wait_ge(const_step, 3)
            G.affine_select(out=ident[:, :], in_=ident[:, :], compare_op=ALU.not_equal, fill=1.0, base=0,
                            pattern=[[-1, P]], channel_multiplier=1)
            G.affine_select(out=tri[:, :], in_=tri[:, :], compare_op=ALU.is_ge, fill=0.0, base=0,
                            pattern=[[1, P]], channel_multiplier=-1)
            G.affine_select(out=strict[:, :], in_=strict[:, :], compare_op=ALU.is_ge, fill=0.0, base=-1,
                            pattern=[[-1, P]], channel_multiplier=1).then_inc(const_ready, 1)
            for hh in range(4):
                G.memset(negslope[:, hh:hh + 1], -(2.0 ** (-8.0 * (hh + 1) / NH)))
            G.memset(neghalf[:, :], -0.5)
            G.iota(dist_i[:, 0:P], pattern=[[-1, P]], base=P, channel_multiplier=1)
            G.iota(dist_i[:, P:3 * P], pattern=[[0, 2], [-1, P]], base=0, channel_multiplier=1).then_inc(const_step, 1)
            pool.wait_ge(const_step, 4)
            G.tensor_copy(dist[:, :], dist_i[:, :]).then_inc(const_step, 1)
            pool.wait_ge(const_step, 5)
            G.affine_select(out=dist[:, P:3 * P], in_=dist[:, P:3 * P], compare_op=ALU.is_ge, fill=1e33, base=0,
                            pattern=[[0, 2], [-1, P]], channel_multiplier=1).then_inc(slope_done, 1)
            pool.wait_ge(slope_done, 1)
            pool.wait_ge(par_ready, 1)
            G.tensor_scalar(par[:, QN_C:QN_C + 1], par[:, QN_C:QN_C + 1], HD ** -0.5, None, ALU.mult) \
                .then_inc(const_ready, 1)
            pool.wait_ge(xms_done, 1)
            G.tensor_tensor(rstd1[:, :], xss[:, :], neghalf[:, 0:2], ALU.pow).then_inc(rstd1_ready, 1)

            def qk_work(g, i, st):
                n = 2 * g + i
                pool.wait_ge(set_free[i], g + 1)
                if later(n):
                    pool.wait_ge(qk_sum, n)
                v = st[:, :, :].rearrange("p t (h d) -> p (t h) d", d=HD)
                G.tensor_tensor(sq[:, :, :], v, v, ALU.mult).then_inc(qk_sq, 1)
                pool.wait_ge(qk_ms, n + 1)
                if later(n):
                    pool.wait_ge(qk_normed, n)
                G.tensor_tensor(rqk[:, :], ssum[:, :], neghalf[:, :], ALU.pow).then_inc(qk_rstd, 1)

            pool.wait_ge(dt_ready, 1)
            qk_work(0, 0, q_st)
            qk_work(0, 1, k_st)
            with pool.Fori(1, 4) as g:
                qk_work(g, 0, q_st)
                qk_work(g, 1, k_st)

            def conv_par(m, cb_):
                if later(m):
                    pool.wait_ge(c_tap, 12 * m)
                G.tensor_copy(cb[:, :], par[:, bass.ds(CB_C + 4 * cb_, 4)])
                for k in range(4):
                    i = G.tensor_copy(cw[:, k, :], par[:, bass.ds(CW_C + 48 * k + 4 * cb_, 4)])
                i.then_inc(c_par, 1)

            for m in range(4):
                conv_par(m, 8 + m)
            with pool.Fori(0, 8) as m:
                conv_par(4 + m, m)

            def ssd(n, c, g):
                if later(n):
                    pool.wait_ge(y_mm, n)
                xg = heads(xs[:, bass.ds(g, 1), c, :].rearrange("p a n -> p (a n)"), HG)
                if c == 0:
                    G.tensor_copy(BTg[:, :], BT[:, bass.ds(g, 1), :].rearrange("p a t -> p (a t)"))
                    G.tensor_copy(CTg[:, :], CT[:, bass.ds(g, 1), :].rearrange("p a t -> p (a t)"))
                    G.tensor_copy(Btg[:, :], Btok[:, bass.ds(g * NST, NST)]).then_inc(g_copied, 1)
                G.tensor_tensor(lm[:, :, :], over(strict[:, :], 1, HG), over(la[:, c, bass.ds(g * HG, HG)], 2, P),
                                ALU.mult).then_inc(lm_ready, 1)
                if c == 0:
                    G.tensor_tensor(xd[:, :, :], xg, over(dtd[:, bass.ds(g * HG, HG)], 2, SHD), ALU.mult)
                G.tensor_tensor(xf[:, :, :], xg, over(dt_[:, c, bass.ds(g * HG, HG)], 2, SHD), ALU.mult) \
                    .then_inc(xf_ready, 1)
                G.tensor_tensor(xg, xg, over(dskip[:, bass.ds(g * HG, HG)], 2, SHD), ALU.mult) \
                    .then_inc(skip_ready, 1)

            def y_rstd(g):
                pool.wait_ge(yms_done, g + 1)
                if later(g):
                    pool.wait_ge(yfin, 2 * g)
                G.tensor_tensor(grs[:, :], gss[:, :], neghalf[:, 0:2], ALU.pow).then_inc(yrs_done, 1)

            pool.wait_ge(c_out, 10)
            pool.wait_ge(dt_ready, 2)
            def ssd_groups(j):
                ssd(4 * j, 0, 2 * j)
                ssd(4 * j + 1, 1, 2 * j)
                y_rstd(2 * j)
                ssd(4 * j + 2, 0, 2 * j + 1)
                ssd(4 * j + 3, 1, 2 * j + 1)
                y_rstd(2 * j + 1)

            ssd_groups(0)
            with pool.Fori(1, 4) as j:
                ssd_groups(j)

            def y_copy(Gn, i):
                pool.wait_ge(yfin, 2 * Gn + 2)
                G.tensor_copy(y_st[i][:, :, :], xs[:, bass.ds(Gn, 1), :, :].rearrange("p a t n -> p (a t) n"))
                G.tensor_copy(sw[i][:, :], par[:, bass.ds(SSM_C + 4 * Gn, 4)]).then_inc(y_copied, 1)

            pool.wait_ge(y_mm, 16)
            pool.wait_ge(yz_done, 8)
            y_copy(0, 0)
            y_copy(1, 1)
            with pool.Fori(1, 4) as j:
                for i in range(2):
                    pool.wait_ge(sT_lo_done, 8 * j - 4 + 4 * i)
                    y_copy(2 * j + i, i)

            with pool.Fori(0, 4) as j:
                pool.wait_ge(m_step, 3 * j + 3)
                G.tensor_tensor(m_st[:, :, :], m_st[:, :, :], merged[:, :, bass.ds(j * COLS, COLS)], ALU.add) \
                    .then_inc(m_ready, 1)
            pool.wait_ge(hms_done, 1)
            G.tensor_tensor(rstd2[:, :], hs2[:, :], neghalf[:, 0:2], ALU.pow).then_inc(rstd2_ready, 1)
            with pool.Fori(0, 4) as q:
                for u in range(4):
                    pool.wait_ge(set_free[u % 2], 27 + 4 * q + u // 2)
                    G.tensor_tensor(r_st[:, :, :], r_st[:, :, :], r_st[:, :, :], ALU.mult).then_inc(r_ready, 1)


_INS = ["x", "mix_norm_w", "w_in", "q_norm_w", "k_norm_w", "conv_w", "conv_b", "dt_bias", "a_log", "d_skip",
        "ssm_norm_w", "w_attn_out", "w_ssm_out", "w_out", "mlp_norm_w", "w_up", "w_down"]


def kernel(**inputs):
    import numpy as np
    import concourse.bacc as bacc
    from concourse.bass_utils import run_bass_kernel_spmd

    nc = bacc.Bacc("TRN2", target_bir_lowering=False, num_devices=1)
    arrays, args = {}, []
    for name in _INS:
        a = np.ascontiguousarray(inputs[name])
        arrays[f"in_{name}"] = a
        args.append(nc.dram_tensor(f"in_{name}", a.shape, mybir.dt.from_np(a.dtype), kind="ExternalInput").ap())
    args.append(nc.dram_tensor("out_h", (1, T, D), mybir.dt.float32, kind="ExternalOutput").ap())
    build(nc, *args)
    r = run_bass_kernel_spmd(nc, [arrays], core_ids=[0])
    return r.results[0]["out_h"]
```

```python
import concourse.bass as bass
from concourse import mybir
from contextlib import ExitStack

D = 2048
T = 256
P = 128
NTOK = T // P
HD = 128
NH = D // HD
INNER = 2 * D
SHD = 64
SNH = INNER // SHD
GROUPS = 8
HG = SNH // GROUPS
GW = INNER // GROUPS
NST = 128
EPS = 1e-6
Q0, K0, V0 = 0, D, 2 * D
Z0 = 3 * D
XBC0 = Z0 + INNER
DT0 = XBC0 + (INNER + 2 * GROUPS * NST)
GATE0 = DT0 + SNH

COLS = 512
KT = D // P
UK = 2
US = KT // UK
SLOTS = 4
LEAD = 3
XLEAD = 4

B_QKV = 0
B_CONV = 12
B_SSD = 24
B_GATE = 40
B_SSM = 44
B_OUT = 52
B_MLP = 56


def build(nc, x, mix_norm_w, w_in, q_norm_w, k_norm_w, conv_w, conv_b, dt_bias, a_log, d_skip, ssm_norm_w,
          w_attn_out, w_ssm_out, w_out, mlp_norm_w, w_up, w_down, out):
    f32 = mybir.dt.float32
    f32r = mybir.dt.float32r
    i32 = mybir.dt.int32
    ALU = mybir.AluOpType
    ACT = mybir.ActivationFunctionType
    AX = mybir.AxisListType

    x, w_in, w_attn_out, w_ssm_out = x[0], w_in[0], w_attn_out[0], w_ssm_out[0]
    w_out, w_up, w_down, out = w_out[0], w_up[0], w_down[0], out[0]

    ctx = ExitStack()
    with ctx:
        BASE = 16512
        KB = 1024
        at = {"RAW": 0, "HI": 16 * KB, "LO": 32 * KB, "A": 48 * KB, "B": 80 * KB, "C": 112 * KB, "D": 144 * KB,
              "E": 164 * KB, "W": 180 * KB}

        def sb(name, region, off, shape, dt=f32):
            return nc.alloc_sbuf_tensor_at(name, shape, dt, offset=BASE + at[region] + off)

        raw = [sb(f"raw{s}", "RAW", 4096 * s, [P, UK, COLS]) for s in range(SLOTS)]
        whi = [sb(f"whi{s}", "HI", 4096 * s, [P, UK, COLS], f32r) for s in range(SLOTS)]
        wlo = [sb(f"wlo{s}", "LO", 4096 * s, [P, UK, COLS], f32r) for s in range(SLOTS)]
        xT_hi = sb("xT_hi", "A", 0, [P, KT, T], f32r)
        xT_lo = sb("xT_lo", "A", 16 * KB, [P, KT, T], f32r)
        gT_hi = sb("gT_hi", "A", 0, [P, KT, T], f32r)
        gT_lo = sb("gT_lo", "A", 16 * KB, [P, KT, T], f32r)
        aT_hi = sb("aT_hi", "B", 0, [P, KT, T], f32r)
        aT_lo = sb("aT_lo", "B", 16 * KB, [P, KT, T], f32r)
        sT_lo = sb("sT_lo", "B", 0, [P, 2 * KT, T], f32r)
        hT_hi = sb("hT_hi", "B", 0, [P, KT, T], f32r)
        hT_lo = sb("hT_lo", "B", 16 * KB, [P, KT, T], f32r)
        q_st = sb("q_st", "C", 0, [P, NTOK, COLS])
        k_st = sb("k_st", "C", 4 * KB, [P, NTOK, COLS])
        v_st = sb("v_st", "C", 8 * KB, [P, NTOK, COLS])
        sq = sb("sq", "C", 12 * KB, [P, 8, HD])
        qT = sb("qT", "C", 16 * KB, [P, 4, T])
        kT = sb("kT", "C", 20 * KB, [P, 4, T])
        prob = sb("prob", "C", 24 * KB, [P, 3 * P])
        probT = sb("probT", "C", 24 * KB + 1536, [P, 3 * P])
        dist = sb("dist", "C", 24 * KB + 3072, [P, 3 * P])
        dist_i = sb("dist_i", "C", 24 * KB + 4608, [P, 3 * P], i32)
        xs = sb("xs", "C", 0, [P, GROUPS, NTOK, GW])
        sT_hi = sb("sT_hi", "C", 0, [P, 2 * KT, T], f32r)
        fT_hi = sb("fT_hi", "C", 0, [P, KT, T], f32r)
        fT_lo = sb("fT_lo", "C", 16 * KB, [P, KT, T], f32r)
        dtw = sb("dtw", "D", 0, [P, KT, SNH])
        dtw_hl = sb("dtw_hl", "D", 4 * KB, [P, KT, 2 * SNH], f32r)
        prow = sb("prow", "D", 12 * KB, [P, 4, P])
        BT = sb("BT", "D", 0, [P, GROUPS, T])
        CT = sb("CT", "D", 8 * KB, [P, GROUPS, T])
        Btok = sb("Btok", "D", 16 * KB, [P, GROUPS * NST])
        sgate = sb("sgate", "D", 0, [P, NTOK, D])
        x_in = sb("x_in", "E", 0, [P, NTOK, D])
        c_st = [sb(f"c_st{i}", "E", 4 * KB * i, [P, NTOK, COLS]) for i in range(2)]
        cacc = sb("cacc", "E", 8 * KB, [P, 4, T])
        cT = sb("cT", "E", 12 * KB, [P, 4, T])
        merged = sb("merged", "E", 0, [P, NTOK, D])
        h = sb("h", "E", 0, [P, NTOK, D])
        tla_hi = sb("tla_hi", "W", 0, [P, HG, P], f32r)
        tla_lo = sb("tla_lo", "W", 8 * KB, [P, HG, P], f32r)
        M = sb("M", "W", 0, [P, HG, P])
        zs = sb("zs", "W", 4 * KB, [P, NTOK, COLS])
        xf = sb("xf", "W", 12 * KB, [P, HG, SHD])
        xd = sb("xd", "W", 14 * KB, [P, HG, SHD])
        prev = sb("prev", "W", 14 * KB, [P, GW])
        yoff = sb("yoff", "W", 16 * KB, [P, HG, SHD])
        BTg = sb("BTg", "W", 18 * KB, [P, T])
        CTg = sb("CTg", "W", 19 * KB, [P, T])
        Btg = sb("Btg", "W", 20 * KB, [P, NST])
        cbm = sb("cbm", "W", 20 * KB + 512, [P, P])
        dtT = sb("dtT", "W", 0, [P, T])
        la = sb("la", "W", 1 * KB, [P, NTOK, SNH])
        y_st = [sb(f"y_st{i}", "W", 4 * KB * i, [P, NTOK, GW]) for i in range(2)]
        s_half = sb("s_half", "W", 0, [P, NTOK, COLS])
        m_st = sb("m_st", "W", 8 * KB, [P, NTOK, COLS])
        r_st = sb("r_st", "W", 0, [P, NTOK, COLS])
        woff = [21 * KB]

        def small(name, shape, dt=f32):
            n = 4
            for s in shape[1:]:
                n *= s
            t = sb(name, "W", woff[0], shape, dt)
            woff[0] += -(-n // 32) * 32
            return t

        ident = small("ident", [P, P])
        tri = small("tri", [P, P])
        strict = small("strict", [P, P])
        strict_r = small("strict_r", [P, P], f32r)
        NPAR = 306
        par = small("par", [P, NPAR])
        MIX_C, MLP_C, SSM_C, CB_C, QN_C, KN_C, CW_C = 0, 16, 32, 64, 112, 113, 114
        negslope = small("negslope", [P, 4])
        neghalf = small("neghalf", [P, 8])
        ssum = small("ssum", [P, 8])
        rqk = small("rqk", [P, 8])
        xss = small("xss", [P, 2])
        rstd1 = small("rstd1", [P, 2])
        negmax = small("negmax", [P, 2])
        psum_ = small("esum", [P, 2])
        pinv = small("pinv", [P, 2])
        dbias = small("dbias", [P, SNH])
        alog = small("alog", [P, SNH])
        dskip = small("dskip", [P, SNH])
        dt_ = small("dt", [P, NTOK, SNH])
        la_hi = small("la_hi", [P, NTOK, SNH], f32r)
        la_lo = small("la_lo", [P, NTOK, SNH], f32r)
        dtd = small("dtd", [P, SNH])
        eac = small("eac", [P, SNH])
        cw = small("cw", [P, 4, 4])
        cb = small("cb", [P, 4])
        gss = small("gss", [P, 2])
        grs = small("grs", [P, 2])
        sw = [small(f"sw{i}", [P, 4]) for i in range(2)]
        hss = small("hss", [P, NTOK, 4])
        hs2 = small("hs2", [P, 2])
        rstd2 = small("rstd2", [P, 2])
        assert BASE + at["W"] + woff[0] <= 229344, (woff[0], 229344 - BASE - at["W"])
        dts = [sb(f"dts{i}", "C", 12 * KB + 512 * i, [P, NTOK, SNH]) for i in range(8)]
        xjunk = [sb(f"xjunk{t}", "B", 8 * KB * t, [P, D]) for t in range(NTOK)]

        X_BANK = [6, 7, 4, 5, 2, 3, 6, 7]

        ps = [ctx.enter_context(nc.psum_tensor(f"ps{i}", [P, 512], f32)) for i in range(8)]
        SETS = [(ps[0], ps[1]), (ps[2], ps[3]), (ps[4], ps[5])]

        def sem(name):
            return ctx.enter_context(nc.semaphore(name))

        raw_in = [sem(f"raw_in{s}") for s in range(SLOTS)]
        hi_ready = sem("hi_ready")
        lo_ready = sem("lo_ready")
        unit_used = sem("unit_used")
        set_free = [sem(f"set_free{k}") for k in range(3)]
        x_loaded = [sem(f"x_loaded{c}") for c in range(4)]
        par_loaded = sem("par_loaded")
        row_loaded = sem("row_loaded")
        dtw_loaded = sem("dtw_loaded")
        const_step = sem("const_step")
        const_ready = sem("const_ready")
        mix_loaded = sem("mix_loaded")
        mix_T = sem("mix_T")
        mix_ready = sem("mix_ready")
        strict_ready = sem("strict_ready")
        par_T = sem("par_T")
        par_ready = sem("par_ready")
        x_T = sem("x_T")
        xT_hi_done = sem("xT_hi_done")
        xT_lo_done = sem("xT_lo_done")
        xsq_done = sem("xsq_done")
        xms_done = sem("xms_done")
        rstd1_ready = sem("rstd1_ready")
        dtw_hi_done = sem("dtw_hi_done")
        dtw_lo_done = sem("dtw_lo_done")
        dt_mm = sem("dt_mm")
        dtT_ready = sem("dtT_ready")
        dt_back = sem("dt_back")
        dt_v = sem("dt_v")
        dt_s = sem("dt_s")
        dec_mm = sem("dec_mm")
        dec_exp = sem("dec_exp")
        dt_ready = sem("dt_ready")
        la_hi_ready = sem("la_hi_ready")
        la_lo_ready = sem("la_lo_ready")
        qk_sq = sem("qk_sq")
        qk_sum = sem("qk_sum")
        qk_ms = sem("qk_ms")
        qk_rstd = sem("qk_rstd")
        qk_normed = sem("qk_normed")
        qk_T = sem("qk_T")
        qkT_ready = sem("qkT_ready")
        scores = sem("scores")
        biased = sem("biased")
        maxed = sem("maxed")
        expd = sem("expd")
        inv_done = sem("inv_done")
        normed = sem("normed")
        p_T = sem("p_T")
        probT_ready = sem("probT_ready")
        pv = sem("pv")
        aT_hi_done = sem("aT_hi_done")
        aT_lo_done = sem("aT_lo_done")
        slope_done = sem("slope_done")
        c_T = sem("c_T")
        c_par = sem("c_par")
        c_first = sem("c_first")
        c_tap = sem("c_tap")
        c_silu = sem("c_silu")
        c_back = sem("c_back")
        c_out = sem("c_out")
        g_copied = sem("g_copied")
        tla_ready = sem("tla_ready")
        xf_ready = sem("xf_ready")
        skip_ready = sem("skip_ready")
        seg_mm = sem("seg_mm")
        cb_mm = sem("cb_mm")
        dec_done = sem("dec_done")
        cbm_done = sem("cbm_done")
        M_ready = sem("M_ready")
        st_mm = sem("st_mm")
        prev_ready = sem("prev_ready")
        off_mm = sem("off_mm")
        y_mm = sem("y_mm")
        yd_done = sem("yd_done")
        yo_done = sem("yo_done")
        y_done = sem("y_done")
        z_sig = sem("z_sig")
        yz_done = sem("yz_done")
        ysq_done = sem("ysq_done")
        yms_done = sem("yms_done")
        yrs_done = sem("yrs_done")
        yfin = sem("yfin")
        y_copied = sem("y_copied")
        y_T = sem("y_T")
        sT_hi_done = sem("sT_hi_done")
        sT_lo_done = sem("sT_lo_done")
        m_step = sem("m_step")
        m_ready = sem("m_ready")
        m_T = sem("m_T")
        gT_hi_done = sem("gT_hi_done")
        gT_lo_done = sem("gT_lo_done")
        x_again = sem("x_again")
        h_sq = sem("h_sq")
        h_T = sem("h_T")
        hT_hi_done = sem("hT_hi_done")
        hT_lo_done = sem("hT_lo_done")
        hsum_done = sem("hsum_done")
        hms_done = sem("hms_done")
        rstd2_ready = sem("rstd2_ready")
        r_ready = sem("r_ready")
        r_T = sem("r_T")
        fT_hi_done = sem("fT_hi_done")
        fT_lo_done = sem("fT_lo_done")
        last_tile0 = sem("last_tile0")
        stored = sem("stored")

        def fp(ap):
            return ap.bitcast(f32)

        def over(ap, axis, n):
            a = ap.unsqueeze(axis)
            shape = list(a.shape)
            shape[axis] = n
            return a.to_broadcast(shape)

        def heads(ap, n):
            return ap.rearrange("p (h d) -> p h d", h=n)

        def later(n):
            return not (isinstance(n, int) and n == 0)

        block = ctx.enter_context(nc.Block())

        @block.sync
        def _(sp):
            def load_params():
                sp.dma_start(dtw[:, :, :], w_in[:, DT0:DT0 + SNH].rearrange("(k p) n -> p k n", p=P)) \
                    .then_inc(dtw_loaded, 16)
                rows = [(mlp_norm_w[0], 16, 0), (ssm_norm_w[0], 32, 16), (conv_b[0], 48, 48), (q_norm_w[0], 1, 96),
                        (k_norm_w[0], 1, 97)]
                for w, n, r in rows:
                    sp.dma_start(prow[r:r + n, 0, :], w.rearrange("(a b) -> a b", b=P)).then_inc(par_loaded, 16)
                for i in range(2):
                    sp.dma_start(prow[0:96, 1 + i, :],
                                  conv_w[0, 2 * i:2 * i + 2, :].rearrange("k (a b) -> (k a) b", b=P)) \
                        .then_inc(par_loaded, 16)
                for w, dst in ((dt_bias, dbias), (a_log, alog), (d_skip, dskip)):
                    sp.dma_start(dst[:, :], w[0].partition_broadcast(P)).then_inc(row_loaded, 16)

            def load_block(b, w, row0, col0, then=None):
                for s in range(US):
                    if not (isinstance(b, int) and b == 0 and s < SLOTS):
                        sp.wait_ge(lo_ready, US * b + s - SLOTS + 1)
                    src = w[bass.ds(row0 + s * UK * P, UK * P), bass.ds(col0, COLS)]
                    sp.dma_start(raw[s % SLOTS][:, :, :], src.rearrange("(k p) n -> p k n", p=P)) \
                        .then_inc(raw_in[s % SLOTS], 16)
                    if then and s == SLOTS - 1:
                        then()

            sp.dma_start(prow[0:KT, 3, :], mix_norm_w[0].rearrange("(a b) -> a b", b=P)).then_inc(mix_loaded, 16)
            load_block(B_QKV, w_in, 0, Q0, then=load_params)
            load_block(B_QKV + 1, w_in, 0, K0)
            load_block(B_QKV + 2, w_in, 0, V0)
            with sp.Fori(1, 4) as g:
                load_block(B_QKV + 3 * g, w_in, 0, Q0 + g * COLS)
                load_block(B_QKV + 3 * g + 1, w_in, 0, K0 + g * COLS)
                load_block(B_QKV + 3 * g + 2, w_in, 0, V0 + g * COLS)
            with sp.Fori(0, 4) as m:
                load_block(B_CONV + m, w_in, 0, XBC0 + INNER + m * COLS)
            with sp.Fori(0, 8) as m:
                load_block(B_CONV + 4 + m, w_in, 0, XBC0 + m * COLS)
            with sp.Fori(1, 5) as j1:
                load_block(B_SSD + 4 * j1 - 4, w_in, 0, Z0 + 2 * j1 * COLS - 2 * COLS)
                load_block(B_SSD + 4 * j1 - 3, w_in, 0, GATE0 + j1 * COLS - COLS)
                load_block(B_SSD + 4 * j1 - 2, w_in, 0, Z0 + 2 * j1 * COLS - COLS)
                load_block(B_SSD + 4 * j1 - 1, w_attn_out, 0, j1 * COLS - COLS)
            with sp.Fori(0, 4) as j:
                load_block(B_GATE + j, w_in, 0, GATE0 + D + j * COLS)
            with sp.Fori(0, 4) as j:
                load_block(B_SSM + 2 * j, w_ssm_out, 0, j * COLS)
                load_block(B_SSM + 2 * j + 1, w_ssm_out, D, j * COLS)
            with sp.Fori(0, 4) as j:
                load_block(B_OUT + j, w_out, 0, j * COLS)
            with sp.Fori(0, 4) as q:
                with sp.Fori(0, 4) as u:
                    load_block(B_MLP + 8 * q + u, w_up, 0, q * D + u * COLS)
                with sp.Fori(0, 4) as d:
                    load_block(B_MLP + 8 * q + 4 + d, w_down, q * D, d * COLS)
            for d in range(3):
                sp.wait_ge(set_free[d % 2], 41 + d // 2)
                sp.dma_start(out[:, d * COLS:(d + 1) * COLS].rearrange("(t p) n -> p t n", p=P),
                             h[:, :, d * COLS:(d + 1) * COLS]).then_inc(stored, 16)
            for t in range(NTOK):
                sp.wait_ge((last_tile0, set_free[1])[t], (1, 42)[t])
                sp.dma_start(out[t * P:(t + 1) * P, 3 * COLS:4 * COLS], h[:, t, 3 * COLS:4 * COLS]) \
                    .then_inc(stored, 16)
            sp.wait_ge(stored, 16 * 5)

        @block.tensor
        def _(pe):
            mm = nc.tensor.matmul

            def transpose(dst, src):
                return nc.tensor.transpose(dst, src, ident[:, :])

            def stream(b, k, uses, hi, lo, kt0=0, ready=None, after=None):
                if later(uses):
                    pe.wait_ge(set_free[k], uses)
                for s in range(US):
                    if ready:
                        ready(s)
                    pe.wait_ge(hi_ready, US * b + s + 1)
                    pe.wait_ge(lo_ready, US * b + s + 1)
                    sl = s % SLOTS
                    for kk in range(UK):
                        kt = kt0 + s * UK + kk
                        for t in range(NTOK):
                            dst = SETS[k][t][:, :]
                            xh = hi[:, kt, t * P:(t + 1) * P]
                            xl = lo[:, kt, t * P:(t + 1) * P]
                            mm(dst, xh, whi[sl][:, kk, :], start=(s == 0 and kk == 0), stop=False)
                            mm(dst, xh, wlo[sl][:, kk, :], start=False, stop=False)
                            last = mm(dst, xl, whi[sl][:, kk, :], start=False, stop=(s == US - 1 and kk == UK - 1))
                    last.then_inc(unit_used, 1)
                    for f in (after or {}).get(s, ()):
                        f()

            pe.wait_ge(const_ready, 1)
            pe.wait_ge(mix_loaded, 16)
            nc.tensor.transpose(ps[0][:, 0:KT], prow[0:KT, 3, :], ident[0:KT, 0:KT]).then_inc(mix_T, 1)

            def x_transposes(i):
                def f():
                    pe.wait_ge(x_loaded[i // 2], 16)
                    if i >= 6:
                        pe.wait_ge(xT_lo_done, 2 * (i - 5))
                    for kk in range(2):
                        for t in range(NTOK):
                            kt = 2 * i + kk
                            last = transpose(ps[X_BANK[i]][:, kk * T + t * P:kk * T + (t + 1) * P],
                                             x_in[:, t, kt * P:(kt + 1) * P])
                    last.then_inc(x_T, 1)
                return f
            for i in range(XLEAD):
                x_transposes(i)()

            def at_transpose(n):
                def f():
                    pe.wait_ge(normed, 2 * n + 2)
                    if later(n):
                        pe.wait_ge(probT_ready, n)
                    transpose(ps[7][:, P:2 * P], prob[:, 0:P])
                    transpose(ps[7][:, 2 * P:3 * P], prob[:, P:2 * P])
                    transpose(ps[7][:, 0:P], prob[:, 2 * P:3 * P]).then_inc(p_T, 1)
                return f

            def at_pv(n, hh, g):
                def f():
                    pe.wait_ge(probT_ready, n + 1)
                    if hh == 0:
                        pe.wait_ge(set_free[2], g + 1)
                    pe.wait_ge(biased, n + 1)
                    mm(ps[6][:, 0:T], v_st[:, 0, hh * HD:(hh + 1) * HD], probT[:, 0:T], start=True, stop=False)
                    mm(ps[6][:, P:T], v_st[:, 1, hh * HD:(hh + 1) * HD], probT[:, T:T + P], start=False,
                       stop=True).then_inc(pv, 1)
                return f

            def attention(g):
                n0 = 4 * g
                a = [{} for _ in range(3)]

                def put(step, f):
                    a[step // 8].setdefault(step % 8, []).append(f)
                put(0, lambda: pe.wait_ge(qkT_ready, 2 * g + 2))
                for hh in range(4):
                    put(6 * hh, at_scores(n0 + hh, hh))
                    put(6 * hh + 2, at_transpose(n0 + hh))
                    put(6 * hh + 4, at_pv(n0 + hh, hh, g))
                return a

            def at_scores(n, hh):
                def f():
                    if later(n):
                        pe.wait_ge(aT_lo_done, n)
                    mm(ps[6][:, 0:T], qT[:, hh, P:T], kT[:, hh, :], start=True, stop=True)
                    mm(ps[6][:, T:T + P], qT[:, hh, 0:P], kT[:, hh, 0:P], start=True, stop=True).then_inc(scores, 1)
                return f

            def qk_transposes(g):
                def f():
                    for i, (st, (ba, bb)) in enumerate(((q_st, SETS[0]), (k_st, SETS[1]))):
                        pe.wait_ge(qk_normed, 2 * g + i + 1)
                        pe.wait_ge(set_free[i], g + 1)
                        for hh in range(4):
                            for t in range(NTOK):
                                o = (hh % 2) * T + t * P
                                last = transpose((ba, bb)[hh // 2][:, o:o + P], st[:, t, hh * HD:(hh + 1) * HD])
                        last.then_inc(qk_T, 1)
                return f

            def par_transposes():
                pe.wait_ge(par_loaded, 16 * 7)
                pe.wait_ge(xT_lo_done, 6)
                nc.tensor.transpose(ps[4][:, 0:CW_C - MLP_C], prow[0:CW_C - MLP_C, 0, :],
                                    ident[0:CW_C - MLP_C, 0:CW_C - MLP_C])
                for i in range(2):
                    last = nc.tensor.transpose(ps[4][:, 128 * (i + 1):128 * (i + 1) + 96], prow[0:96, 1 + i, :],
                                               ident[0:96, 0:96])
                last.then_inc(par_T, 1)

            def dt_matmuls():
                pe.wait_ge(dtw_hi_done, 1)
                pe.wait_ge(dtw_lo_done, 1)
                mm(ps[6][:, 0:T], dtw_hl[:, 0, :], xT_hi[:, 0, :], start=True, stop=False)
                for kt in range(KT):
                    mm(ps[6][0:SNH, 0:T], dtw_hl[:, kt, 0:SNH], xT_lo[:, kt, :], start=False, stop=False)
                for kt in range(1, KT):
                    last = mm(ps[6][:, 0:T], dtw_hl[:, kt, :], xT_hi[:, kt, :], start=False, stop=(kt == KT - 1))
                last.then_inc(dt_mm, 1)

            def dt_transposes():
                pe.wait_ge(dtT_ready, 1)
                for t in range(NTOK):
                    last = transpose(ps[7][:, t * P:(t + 1) * P], dtT[:, t * P:(t + 1) * P])
                last.then_inc(dt_back, 1)

            def decay_matmuls():
                pe.wait_ge(dt_ready, 1)
                mm(ps[6][:, 0:SNH], strict[:, :], la[:, 0, :], start=True, stop=True)
                mm(ps[6][:, SNH:2 * SNH], tri[:, :], la[:, 1, :], start=True, stop=True).then_inc(dec_mm, 1)

            pe.wait_ge(mix_ready, 1)
            a = {s: [x_transposes(XLEAD + s)] for s in range(US - XLEAD)}
            a[6] = [par_transposes]
            stream(B_QKV, 0, 0, xT_hi, xT_lo, ready=lambda s: pe.wait_ge(xT_lo_done, 2 * s + 2), after=a)
            stream(B_QKV + 1, 1, 0, xT_hi, xT_lo, after={0: [dt_matmuls], 1: [dt_transposes]})
            pe.wait_ge(par_ready, 1)
            stream(B_QKV + 2, 2, 0, xT_hi, xT_lo, after={1: [decay_matmuls], 4: [qk_transposes(0)]})
            pe.wait_ge(dec_exp, 1)
            def qkv_group(g):
                a = attention(g - 1)
                a[2].setdefault(4, []).insert(0, qk_transposes(g))
                pe.wait_ge(qkT_ready, 2 * g - 1)
                stream(B_QKV + 3 * g, 0, g, xT_hi, xT_lo, after=a[0])
                pe.wait_ge(qkT_ready, 2 * g)
                stream(B_QKV + 3 * g + 1, 1, g, xT_hi, xT_lo, after=a[1])
                stream(B_QKV + 3 * g + 2, 2, g, xT_hi, xT_lo, after=a[2])

            qkv_group(1)
            with pe.Fori(2, 4) as g:
                qkv_group(g)

            def conv_T(m, i, staged, backs):
                def f():
                    pe.wait_ge(set_free[i], staged)
                    if later(m):
                        pe.wait_ge(c_silu, m)
                        pe.wait_ge(c_out, backs)
                    else:
                        pe.wait_ge(set_free[2], 4)
                    for c in range(4):
                        for t in range(NTOK):
                            o = (c % 2) * T + t * P
                            last = transpose(ps[4 + c // 2][:, o:o + P], c_st[i][:, t, c * P:(c + 1) * P])
                    last.then_inc(c_T, 1)
                return f

            def conv_back(m, src, chunks):
                def f():
                    pe.wait_ge(c_silu, m + 1)
                    for t in range(chunks):
                        for c in range(4):
                            last = transpose(ps[4 + t][:, c * P:(c + 1) * P], src[:, c, t * P:(t + 1) * P])
                    last.then_inc(c_back, 1)
                return f

            a = attention(3)

            def conv_after(m, i, staged, backs, src=None, chunks=2, more=None):
                d = dict(more or {})
                d[1] = d.get(1, []) + [conv_T(m, i, staged, backs)]
                if src is not None:
                    d[6] = d.get(6, []) + [conv_back(m, src, chunks)]
                return d

            pe.wait_ge(qkT_ready, 7)
            stream(B_CONV, 0, 4, xT_hi, xT_lo, after=a[0])
            pe.wait_ge(qkT_ready, 8)
            stream(B_CONV + 1, 1, 4, xT_hi, xT_lo, after=conv_after(0, 0, 5, 0, BT[:, 0:4, :], 1, a[1]))
            stream(B_CONV + 2, 0, 5, xT_hi, xT_lo, after=conv_after(1, 1, 5, 1, BT[:, 4:8, :], 1, a[2]))
            stream(B_CONV + 3, 1, 5, xT_hi, xT_lo, after=conv_after(2, 0, 6, 2))
            stream(B_CONV + 4, 0, 6, xT_hi, xT_lo, after=conv_after(3, 1, 6, 2))
            with pe.Fori(0, 3) as i:
                stream(B_CONV + 5 + 2 * i, 1, 6 + i, xT_hi, xT_lo, after=conv_after(4 + 2 * i, 0, 7 + i, 2 + 2 * i, cT))
                stream(B_CONV + 6 + 2 * i, 0, 7 + i, xT_hi, xT_lo, after=conv_after(5 + 2 * i, 1, 7 + i, 3 + 2 * i, cT))
            stream(B_CONV + 11, 1, 9, xT_hi, xT_lo, after=conv_after(10, 0, 10, 8, cT))

            def ssd_state(n, c, g):
                def f():
                    pe.wait_ge(xf_ready, n + 1)
                    if c == 0:
                        if later(g):
                            pe.wait_ge(yo_done, g)
                        mm(ps[7][:, :], Btg[:, :], xd[:, :, :].rearrange("p h d -> p (h d)"), start=True,
                           stop=True).then_inc(st_mm, 1)
                    else:
                        pe.wait_ge(prev_ready, g + 1)
                        mm(ps[7][:, :], CTg[:, P:T], prev[:, :], start=True, stop=True).then_inc(off_mm, 1)
                return f

            def ssd_y(n, c, g):
                def f():
                    pe.wait_ge(M_ready, n + 1)
                    for hh in range(HG):
                        last = mm(ps[6][:, hh * SHD:(hh + 1) * SHD], M[:, hh, :], xf[:, hh, :], start=True,
                                  stop=True)
                    last.then_inc(y_mm, 1)
                return f

            def ssd_after(n, c, g):
                def seg():
                    pe.wait_ge(g_copied, g + 1)
                    if later(n):
                        pe.wait_ge(yd_done, n)
                    mm(ps[6][:, 0:P], BTg[:, c * P:(c + 1) * P], CTg[:, c * P:(c + 1) * P], start=True,
                       stop=True).then_inc(cb_mm, 1)
                    pe.wait_ge(tla_ready, n + 1)
                    for i in range(2):
                        dst = ps[4 + i][:, :]
                        for k, part in enumerate((tla_hi, tla_lo)):
                            last = mm(dst, strict_r[:, :], part[:, 4 * i:4 * i + 4, :].rearrange("p h l -> p (h l)"),
                                      start=(k == 0), stop=(k == 1))
                        last.then_inc(seg_mm, 1)
                if later(n):
                    return {1: [seg], 2: [ssd_state(n, c, g)], 4: [ssd_y(n, c, g)]}

                def banks_free():
                    pe.wait_ge(c_out, 10)
                    pe.wait_ge(aT_lo_done, NH)
                    pe.wait_ge(strict_ready, 1)
                return {0: [conv_T(11, 1, 10, 9)], 3: [conv_back(11, cT, 2)], 5: [banks_free, seg],
                        6: [ssd_state(n, c, g)], 7: [ssd_y(n, c, g)]}

            def ssd_blocks(j):
                b = B_SSD + 4 * j
                stream(b, 0, 10 + 2 * j, xT_hi, xT_lo, after=ssd_after(4 * j, 0, 2 * j))
                stream(b + 1, 1, 10 + 2 * j, xT_hi, xT_lo, after=ssd_after(4 * j + 1, 1, 2 * j))
                stream(b + 2, 0, 11 + 2 * j, xT_hi, xT_lo, after=ssd_after(4 * j + 2, 0, 2 * j + 1))
                stream(b + 3, 1, 11 + 2 * j, aT_hi, aT_lo, after=ssd_after(4 * j + 3, 1, 2 * j + 1))

            ssd_blocks(0)
            with pe.Fori(1, 4) as j:
                ssd_blocks(j)

            def y_transposes(G, i):
                def f():
                    pe.wait_ge(y_copied, G + 1)
                    for c in range(4):
                        for t in range(NTOK):
                            o = (c % 2) * T + t * P
                            last = transpose(ps[4 + 2 * i + c // 2][:, o:o + P], y_st[i][:, t, c * P:(c + 1) * P])
                    last.then_inc(y_T, 1)
                return f

            with pe.Fori(0, 2) as i:
                for k in range(2):
                    jb = 2 * i + k
                    G = 2 * jb
                    stream(B_GATE + jb, k, 18 + i, xT_hi, xT_lo,
                           after={2: [y_transposes(G, 0)], 6: [y_transposes(G + 1, 1)]})

            def m_transposes(j):
                def f():
                    pe.wait_ge(m_ready, j + 1)
                    if later(j):
                        pe.wait_ge(gT_lo_done, 2 * j)
                    for c in range(4):
                        for t in range(NTOK):
                            o = (c % 2) * T + t * P
                            last = transpose(ps[4 + c // 2][:, o:o + P], m_st[:, t, c * P:(c + 1) * P])
                    last.then_inc(m_T, 1)
                return f

            stream(B_SSM, 0, 20, sT_hi, sT_lo, ready=lambda s: pe.wait_ge(sT_lo_done, 2 * s + 2))
            stream(B_SSM + 1, 1, 20, sT_hi, sT_lo, kt0=KT, ready=lambda s: pe.wait_ge(sT_lo_done, KT + 2 * s + 2))
            def ssm_out(j):
                stream(B_SSM + 2 * j, 0, 20 + j, sT_hi, sT_lo, after={3: [m_transposes(j - 1)]})
                stream(B_SSM + 2 * j + 1, 1, 20 + j, sT_hi, sT_lo, kt0=KT)
            ssm_out(1)
            with pe.Fori(2, 4) as j:
                ssm_out(j)

            def h_transposes(j):
                def f():
                    pe.wait_ge(set_free[j % 2], 25 + j // 2)
                    ba = 6 if j % 2 == 0 else 4
                    if j == 1:
                        pe.wait_ge(gT_lo_done, 8)
                    if j >= 2:
                        pe.wait_ge(hT_lo_done, 4 * (j - 1))
                    for c in range(4):
                        for t in range(NTOK):
                            o = (c % 2) * T + t * P
                            last = transpose(ps[ba + c // 2][:, o:o + P],
                                             h[:, t, j * COLS + c * P:j * COLS + (c + 1) * P])
                    last.then_inc(h_T, 1)
                return f

            def merged_ready(s):
                if s == 0:
                    pe.wait_ge(gT_lo_done, 6)
                if s == 6:
                    pe.wait_ge(gT_lo_done, 8)
            stream(B_OUT, 0, 24, gT_hi, gT_lo, ready=merged_ready, after={2: [m_transposes(3)]})
            for j in range(1, 4):
                stream(B_OUT + j, j % 2, 24 + j // 2, gT_hi, gT_lo, after={2: [h_transposes(j - 1)]})

            def r_transposes(q, u):
                def f():
                    n = 4 * q + u
                    pe.wait_ge(r_ready, n + 1)
                    ba = 4 + 2 * (u % 2)
                    if not (isinstance(n, int) and n < 2):
                        pe.wait_ge(fT_lo_done, 2 * n - 2)
                    for c in range(4):
                        for t in range(NTOK):
                            o = (c % 2) * T + t * P
                            last = transpose(ps[ba + c // 2][:, o:o + P], r_st[:, t, c * P:(c + 1) * P])
                    last.then_inc(r_T, 1)
                return f

            def h_ready(s):
                if s == 0:
                    pe.wait_ge(hT_lo_done, 12)
                if s == 6:
                    pe.wait_ge(hT_lo_done, KT)

            def mlp(q):
                b = B_MLP + 8 * q
                for u in range(4):
                    if later(q) or u:
                        stream(b + u, u % 2, 26 + 4 * q + u // 2, hT_hi, hT_lo,
                               after={3: [r_transposes(q, u - 1)]} if u else None)
                    else:
                        stream(b, 0, 26, hT_hi, hT_lo, ready=h_ready, after={1: [h_transposes(3)]})

                def ff_ready(s):
                    if s == 0:
                        pe.wait_ge(fT_lo_done, 8 * q + 6)
                    if s == 6:
                        pe.wait_ge(fT_lo_done, 8 * q + 8)
                stream(b + 4, 0, 28 + 4 * q, fT_hi, fT_lo, ready=ff_ready, after={3: [r_transposes(q, 3)]})
                for d in range(1, 4):
                    stream(b + 4 + d, d % 2, 28 + 4 * q + d // 2, fT_hi, fT_lo)

            mlp(0)
            with pe.Fori(1, 4) as q:
                mlp(q)

        @block.scalar
        def _(act):
            A = nc.scalar.activation

            def split(b, s):
                if s >= US:
                    b, s = b + 1, s - US
                act.wait_ge(raw_in[s % SLOTS], 16 * ((US // SLOTS) * b + s // SLOTS + 1))
                if not (isinstance(b, int) and b == 0 and s < SLOTS):
                    act.wait_ge(unit_used, US * b + s - SLOTS + 1)
                A(whi[s % SLOTS][:, :, :], raw[s % SLOTS][:, :, :], ACT.Copy).then_inc(hi_ready, 1)

            def steps(b, work=None, last=False):
                for s in range(US):
                    if not (last and s + LEAD >= US):
                        split(b, s + LEAD)
                    for f in (work or {}).get(s, ()):
                        f()

            def block_done(b):
                act.wait_ge(unit_used, US * b + US)

            for c in range(4):
                act.dma_start(x_in[:, :, c * COLS:(c + 1) * COLS],
                              x[:, c * COLS:(c + 1) * COLS].rearrange("(t p) n -> p t n", p=P)) \
                    .then_inc(x_loaded[c], 16)
            act.wait_ge(const_ready, 1)
            A(strict_r[:, :], strict[:, :], ACT.Copy).then_inc(strict_ready, 1)
            act.wait_ge(mix_T, 1)
            A(par[:, 0:KT], ps[0][:, 0:KT], ACT.Copy).then_inc(mix_ready, 1)
            act.wait_ge(mix_ready, 1)

            def x_hi(i):
                def f():
                    act.wait_ge(x_T, i + 1)
                    for kk in range(2):
                        kt = 2 * i + kk
                        A(xT_hi[:, kt, :], ps[X_BANK[i]][:, kk * T:(kk + 1) * T], ACT.Copy,
                          scale=par[:, MIX_C + kt:MIX_C + kt + 1]).then_inc(xT_hi_done, 1)
                return f
            for i in range(XLEAD):
                x_hi(i)()
                if i < LEAD:
                    split(0, i)

            def x_squares():
                for t in range(NTOK):
                    A(xjunk[t][:, :], x_in[:, t, :], ACT.Square, accum_out=xss[:, t:t + 1]).then_inc(xsq_done, 1)

            def dtw_round():
                act.wait_ge(dtw_loaded, 16)
                A(dtw_hl[:, :, 0:SNH], dtw[:, :, :], ACT.Copy).then_inc(dtw_hi_done, 1)

            def par_copy():
                act.wait_ge(par_T, 1)
                A(par[:, MLP_C:CW_C], ps[4][:, 0:CW_C - MLP_C], ACT.Copy)
                A(par[:, CW_C:CW_C + 96], ps[4][:, 128:224], ACT.Copy)
                A(par[:, CW_C + 96:NPAR], ps[4][:, 256:352], ACT.Copy).then_inc(par_ready, 1)

            def evac_qk(g, i, st):
                def f():
                    block_done(B_QKV + 3 * g + i)
                    if isinstance(g, int) and g == 0:
                        act.wait_ge(rstd1_ready, 1)
                    else:
                        act.wait_ge(qk_T, 2 * g - 1 + i)
                    A(st[:, 0, :], SETS[i][0][:, :], ACT.Copy, scale=rstd1[:, 0:1])
                    A(st[:, 1, :], SETS[i][1][:, :], ACT.Copy, scale=rstd1[:, 1:2]).then_inc(set_free[i], 1)
                return f

            def evac_v(g):
                def f():
                    block_done(B_QKV + 3 * g + 2)
                    if later(g):
                        act.wait_ge(pv, 4 * g)
                    A(v_st[:, 0, :], SETS[2][0][:, :], ACT.Copy, scale=rstd1[:, 0:1])
                    A(v_st[:, 1, :], SETS[2][1][:, :], ACT.Copy, scale=rstd1[:, 1:2]).then_inc(set_free[2], 1)
                return f

            def evac_qkT(g):
                def f():
                    for i, (dst, w) in enumerate(((qT, QN_C), (kT, KN_C))):
                        act.wait_ge(qk_T, 2 * g + i + 1)
                        act.wait_ge(const_ready, 2)
                        if later(g):
                            act.wait_ge(scores, 4 * g)
                        A(dst[:, 0:2, :], heads(SETS[i][0][:, :], 2), ACT.Copy, scale=par[:, w:w + 1])
                        A(dst[:, 2:4, :], heads(SETS[i][1][:, :], 2), ACT.Copy, scale=par[:, w:w + 1]) \
                            .then_inc(qkT_ready, 1)
                return f

            def at_exp(n):
                def f():
                    act.wait_ge(maxed, 2 * n + 2)
                    if later(n):
                        act.wait_ge(normed, 2 * n)
                    A(prob[:, 0:T], prob[:, 0:T], ACT.Exp, bias=negmax[:, 0:1], accum_out=psum_[:, 0:1])
                    A(prob[:, T:T + P], prob[:, T:T + P], ACT.Exp, bias=negmax[:, 1:2],
                      accum_out=psum_[:, 1:2]).then_inc(expd, 1)
                return f

            def at_copy(n):
                def f():
                    act.wait_ge(p_T, n + 1)
                    if later(n):
                        act.wait_ge(pv, n)
                    A(probT[:, :], ps[7][:, 0:3 * P], ACT.Copy).then_inc(probT_ready, 1)
                return f

            def at_hi(n):
                def f():
                    act.wait_ge(pv, n + 1)
                    A(aT_hi[:, bass.ds(n, 1), :].rearrange("p a t -> p (a t)"), ps[6][:, 0:T], ACT.Copy) \
                        .then_inc(aT_hi_done, 1)
                return f

            def attention(n0):
                a = [{} for _ in range(3)]

                def put(step, f):
                    a[step // 8].setdefault(step % 8, []).append(f)
                for hh in range(4):
                    put(6 * hh + 1, at_exp(n0 + hh))
                    put(6 * hh + 2, at_copy(n0 + hh))
                    put(6 * hh + 4, at_hi(n0 + hh))
                return a

            def dt_chain():
                act.wait_ge(dt_back, 1)
                act.wait_ge(rstd1_ready, 1)
                for t in range(NTOK):
                    A(dts[0][:, t, :], ps[7][:, t * P:t * P + SNH], ACT.Copy, scale=rstd1[:, t:t + 1])
                    i = A(dts[6][:, t, :], ps[7][:, t * P + SNH:(t + 1) * P], ACT.Copy, scale=rstd1[:, t:t + 1])
                i.then_inc(dt_s, 1)
                act.wait_ge(dt_v, 4)
                A(dts[3][:, :, :], dts[2][:, :, :], ACT.Exp).then_inc(dt_s, 1)
                act.wait_ge(dt_v, 5)
                A(dts[5][:, :, :], dts[4][:, :, :], ACT.Ln).then_inc(dt_s, 1)
                act.wait_ge(row_loaded, 48)
                A(alog[:, :], alog[:, :], ACT.Exp).then_inc(dt_s, 1)
                act.wait_ge(dt_ready, 1)
                A(la_hi[:, :, :], la[:, :, :], ACT.Copy).then_inc(la_hi_ready, 1)

            def dtT_copy():
                act.wait_ge(dt_mm, 1)
                A(dtT[:, :], ps[6][:, 0:T], ACT.Copy).then_inc(dtT_ready, 1)

            def dec_chain():
                act.wait_ge(dec_mm, 1)
                A(dtd[:, :], ps[6][:, 0:SNH], ACT.Exp)
                A(eac[:, :], ps[6][:, SNH:2 * SNH], ACT.Exp).then_inc(dec_exp, 1)

            def add(d, step, f):
                d.setdefault(step, []).append(f)
                return d

            w = {s: [x_hi(XLEAD + s)] for s in range(US - XLEAD)}
            w[5] = [x_squares, dtw_round]
            w[7] = [par_copy, evac_qk(0, 0, q_st)]
            steps(B_QKV, w)
            steps(B_QKV + 1, {1: [dtT_copy], 2: [dt_chain], 7: [evac_qk(0, 1, k_st)]})
            steps(B_QKV + 2, {1: [dec_chain], 4: [evac_qkT(0)], 7: [evac_v(0)]})
            def qkv_group(g):
                a = attention(4 * g - 4)
                steps(B_QKV + 3 * g, add(a[0], 7, evac_qk(g, 0, q_st)))
                steps(B_QKV + 3 * g + 1, add(a[1], 7, evac_qk(g, 1, k_st)))
                a[2].setdefault(4, []).insert(0, evac_qkT(g))
                steps(B_QKV + 3 * g + 2, add(a[2], 7, evac_v(g)))

            qkv_group(1)
            with act.Fori(2, 4) as g:
                qkv_group(g)

            def conv_evac(m, k, i):
                def f():
                    block_done(B_CONV + m)
                    if not (isinstance(m, int) and m < 2):
                        act.wait_ge(c_T, m - 1)
                    A(c_st[i][:, 0, :], SETS[k][0][:, :], ACT.Copy, scale=rstd1[:, 0:1])
                    A(c_st[i][:, 1, :], SETS[k][1][:, :], ACT.Copy, scale=rstd1[:, 1:2]).then_inc(set_free[k], 1)
                return f

            def conv_first(m):
                def f():
                    act.wait_ge(c_T, m + 1)
                    act.wait_ge(c_par, m + 1)
                    if later(m):
                        act.wait_ge(c_silu, m)
                    for c in range(4):
                        i = A(cacc[:, c, :], ps[4 + c // 2][:, (c % 2) * T:(c % 2 + 1) * T], ACT.Identity,
                              scale=cw[:, 3, c:c + 1], bias=cb[:, c:c + 1])
                        if c % 2:
                            i.then_inc(c_first, 1)
                return f

            def conv_silu(m, dst):
                def f():
                    act.wait_ge(c_tap, 12 * m + 12)
                    A(dst, cacc[:, :, :], ACT.Silu).then_inc(c_silu, 1)
                return f

            def conv_out(m, kind):
                def f():
                    if kind != "C":
                        act.wait_ge(c_back, back_count(m))
                    if kind == "B":
                        A(Btok[:, m * COLS:(m + 1) * COLS], ps[4][:, :], ACT.Copy).then_inc(c_out, 1)
                    if kind == "x":
                        g = m - 4
                        A(xs[:, bass.ds(g, 1), 0, :].rearrange("p a n -> p (a n)"), ps[4][:, :], ACT.Copy)
                        A(xs[:, bass.ds(g, 1), 1, :].rearrange("p a n -> p (a n)"), ps[5][:, :], ACT.Copy) \
                            .then_inc(c_out, 1)
                return f

            def back_count(m):
                return m + 1 if isinstance(m, int) and m < 2 else m - 1

            def conv_work(m, dst, kind, evac_f, more=None):
                d = dict(more or {})
                add(d, 1, conv_first(m))
                add(d, 4, conv_silu(m, dst))
                if kind != "C":
                    add(d, 6, conv_out(m, kind))
                if evac_f:
                    add(d, 7, evac_f)
                return d

            a = attention(12)
            steps(B_CONV, add(a[0], 7, conv_evac(0, 0, 0)))
            steps(B_CONV + 1, conv_work(0, BT[:, 0:4, :], "B", conv_evac(1, 1, 1), a[1]))
            steps(B_CONV + 2, conv_work(1, BT[:, 4:8, :], "B", conv_evac(2, 0, 0), a[2]))
            steps(B_CONV + 3, conv_work(2, CT[:, 0:4, :], "C", conv_evac(3, 1, 1)))
            steps(B_CONV + 4, conv_work(3, CT[:, 4:8, :], "C", conv_evac(4, 0, 0)))
            with act.Fori(0, 3) as i:
                steps(B_CONV + 5 + 2 * i, conv_work(4 + 2 * i, cT[:, :, :], "x", conv_evac(5 + 2 * i, 1, 1)))
                steps(B_CONV + 6 + 2 * i, conv_work(5 + 2 * i, cT[:, :, :], "x", conv_evac(6 + 2 * i, 0, 0)))
            steps(B_CONV + 11, conv_work(10, cT[:, :, :], "x", conv_evac(11, 1, 1)))

            def ssd_exp(n):
                def f():
                    for i in range(2):
                        act.wait_ge(seg_mm, 2 * n + i + 1)
                        A(M[:, 4 * i:4 * i + 4, :], heads(ps[4 + i][:, :], 4), ACT.Exp).then_inc(dec_done, 1)
                return f

            def ssd_prev(g):
                def f():
                    act.wait_ge(st_mm, g + 1)
                    if later(g):
                        act.wait_ge(off_mm, g)
                    A(prev[:, :], ps[7][:, :], ACT.Copy).then_inc(prev_ready, 1)
                return f

            def z_sigmoid(b, g):
                def f():
                    block_done(b)
                    if later(g):
                        act.wait_ge(yz_done, g)
                        act.wait_ge(ysq_done, 2 * g)
                    for t in range(NTOK):
                        A(zs[:, t, :], SETS[0][t][:, :], ACT.Sigmoid, scale=rstd1[:, t:t + 1]).then_inc(z_sig, 1)
                return f

            def agate(b, j):
                def f():
                    block_done(b)
                    for t in range(NTOK):
                        i = A(merged[:, t, bass.ds(j * COLS, COLS)], SETS[1][t][:, :], ACT.Sigmoid,
                              scale=rstd1[:, t:t + 1])
                    i.then_inc(set_free[1], 1)
                return f

            def y_squares(g):
                def f():
                    act.wait_ge(yz_done, g + 1)
                    if later(g):
                        act.wait_ge(yrs_done, g)
                    for t in range(NTOK):
                        A(zs[:, t, :], xs[:, bass.ds(g, 1), t, :].rearrange("p a n -> p (a n)"), ACT.Square,
                          accum_out=gss[:, t:t + 1]).then_inc(ysq_done, 1)
                return f

            def ssd_blocks(j):
                b = B_SSD + 4 * j
                n = 4 * j
                g = 2 * j
                if later(j):
                    steps(b, {2: [ssd_exp(n)], 3: [ssd_prev(g)], 7: [z_sigmoid(b, g)]})
                else:
                    steps(b, {1: [conv_first(11)], 3: [conv_silu(11, cT[:, :, :])], 4: [conv_out(11, "x")],
                              6: [ssd_exp(n)], 7: [ssd_prev(g), z_sigmoid(b, g)]})
                steps(b + 1, {2: [ssd_exp(n + 1)], 6: [y_squares(g)], 7: [agate(b + 1, j)]})
                steps(b + 2, {2: [ssd_exp(n + 2)], 3: [ssd_prev(g + 1)], 7: [z_sigmoid(b + 2, g + 1)]})
                steps(b + 3, {2: [ssd_exp(n + 3)], 6: [y_squares(g + 1)]})

            ssd_blocks(0)
            with act.Fori(1, 4) as j:
                ssd_blocks(j)

            def sgate_evac(b, k, j):
                def f():
                    block_done(b)
                    for t in range(NTOK):
                        i = A(sgate[:, t, bass.ds(j * COLS, COLS)], SETS[k][t][:, :], ACT.Sigmoid,
                              scale=rstd1[:, t:t + 1])
                    i.then_inc(set_free[k], 1)
                return f

            def s_hi(G, i):
                def f():
                    act.wait_ge(y_T, G + 1)
                    for c in range(4):
                        A(sT_hi[:, bass.ds(4 * G + c, 1), :].rearrange("p a t -> p (a t)"),
                          ps[4 + 2 * i + c // 2][:, (c % 2) * T:(c % 2 + 1) * T], ACT.Copy,
                          scale=sw[i][:, c:c + 1]).then_inc(sT_hi_done, 1)
                return f

            with act.Fori(0, 2) as i:
                for k in range(2):
                    jb = 2 * i + k
                    steps(B_GATE + jb, {2: [s_hi(2 * jb, 0)], 6: [s_hi(2 * jb + 1, 1)],
                                        7: [sgate_evac(B_GATE + jb, k, jb)]})

            def half_evac(j):
                def f():
                    block_done(B_SSM + 2 * j)
                    if later(j):
                        act.wait_ge(m_step, 3 * j)
                    for t in range(NTOK):
                        i = A(s_half[:, t, :], SETS[0][t][:, :], ACT.Copy)
                    i.then_inc(set_free[0], 1)
                return f

            def g_hi(j):
                def f():
                    act.wait_ge(m_T, j + 1)
                    for i in range(2):
                        A(gT_hi[:, bass.ds(4 * j + 2 * i, 2), :], heads(ps[4 + i][:, :], 2), ACT.Copy) \
                            .then_inc(gT_hi_done, 1)
                return f

            steps(B_SSM, {7: [half_evac(0)]})
            steps(B_SSM + 1)
            with act.Fori(1, 4) as j:
                steps(B_SSM + 2 * j, {3: [g_hi(j - 1)], 7: [half_evac(j)]})
                steps(B_SSM + 2 * j + 1)

            def reload_x():
                act.wait_ge(m_ready, 4)
                act.dma_start(h[:, :, :], x.rearrange("(t p) n -> p t n", p=P)).then_inc(x_again, 16)

            def h_squares(j):
                def f():
                    act.wait_ge(set_free[j % 2], 25 + j // 2)
                    act.wait_ge(h_sq, 2 * j)
                    for t in range(NTOK):
                        A(zs[:, t, :], h[:, t, j * COLS:(j + 1) * COLS], ACT.Square,
                          accum_out=hss[:, t, j:j + 1]).then_inc(h_sq, 1)
                return f

            def h_hi(j):
                def f():
                    act.wait_ge(h_T, j + 1)
                    ba = 6 if j % 2 == 0 else 4
                    for c in range(4):
                        kt = 4 * j + c
                        A(hT_hi[:, kt, :], ps[ba + c // 2][:, (c % 2) * T:(c % 2 + 1) * T], ACT.Copy,
                          scale=par[:, MLP_C + kt:MLP_C + kt + 1]).then_inc(hT_hi_done, 1)
                return f

            steps(B_OUT, {2: [g_hi(3), reload_x]})
            for j in range(1, 4):
                steps(B_OUT + j, {1: [h_squares(j - 1)], 2: [h_hi(j - 1)]})

            def relu(b, k, n):
                def f():
                    block_done(b)
                    if later(n):
                        act.wait_ge(r_T, n)
                    else:
                        act.wait_ge(rstd2_ready, 1)
                    for t in range(NTOK):
                        i = A(r_st[:, t, :], SETS[k][t][:, :], ACT.Relu, scale=rstd2[:, t:t + 1])
                    i.then_inc(set_free[k], 1)
                return f

            def f_hi(n, u):
                def f():
                    act.wait_ge(r_T, n + 1)
                    for i in range(2):
                        A(fT_hi[:, 4 * u + 2 * i:4 * u + 2 * i + 2, :], heads(ps[4 + 2 * (u % 2) + i][:, :], 2),
                          ACT.Copy).then_inc(fT_hi_done, 1)
                return f

            def mlp(q, end=False):
                b = B_MLP + 8 * q
                for u in range(4):
                    w = {7: [relu(b + u, u % 2, 4 * q + u)]}
                    if not later(q) and u == 0:
                        w[1] = [h_hi(3), h_squares(3)]
                    if u:
                        w[3] = [f_hi(4 * q + u - 1, u - 1)]
                    steps(b + u, w)
                steps(b + 4, {3: [f_hi(4 * q + 3, 3)]})
                for d in range(1, 4):
                    steps(b + 4 + d, last=end and d == 3)

            mlp(0)
            with act.Fori(1, 3) as q:
                mlp(q)
            mlp(3, end=True)

        @block.vector
        def _(dve):
            V = nc.vector

            def split(b, s):
                if s >= US:
                    b, s = b + 1, s - US
                dve.wait_ge(hi_ready, US * b + s + 1)
                V.tensor_tensor(wlo[s % SLOTS][:, :, :], raw[s % SLOTS][:, :, :], fp(whi[s % SLOTS][:, :, :]),
                                ALU.subtract).then_inc(lo_ready, 1)

            def steps(b, work=None, last=False):
                for s in range(US):
                    if not (last and s + LEAD >= US):
                        split(b, s + LEAD)
                    for f in (work or {}).get(s, ()):
                        f()

            def block_done(b):
                dve.wait_ge(unit_used, US * b + US)

            dve.wait_ge(mix_ready, 1)

            def x_lo(i):
                def f():
                    dve.wait_ge(xT_hi_done, 2 * i + 2)
                    for kk in range(2):
                        kt = 2 * i + kk
                        V.scalar_tensor_tensor(xT_lo[:, kt, :], ps[X_BANK[i]][:, kk * T:(kk + 1) * T],
                                               par[:, MIX_C + kt:MIX_C + kt + 1], fp(xT_hi[:, kt, :]), ALU.mult,
                                               ALU.subtract).then_inc(xT_lo_done, 1)
                return f
            for i in range(XLEAD):
                x_lo(i)()
                if i < LEAD:
                    split(0, i)

            def dtw_rest():
                dve.wait_ge(dtw_hi_done, 1)
                V.tensor_tensor(dtw_hl[:, :, SNH:2 * SNH], dtw[:, :, :], fp(dtw_hl[:, :, 0:SNH]), ALU.subtract) \
                    .then_inc(dtw_lo_done, 1)

            def x_mean():
                dve.wait_ge(xsq_done, 2)
                V.tensor_scalar(xss[:, :], xss[:, :], 1.0 / D, EPS, ALU.mult, ALU.add).then_inc(xms_done, 1)

            dtc = [0]

            def link(ins):
                dtc[0] += 1
                ins.then_inc(dt_v, 1)
                return dtc[0]

            def dt_chain():
                X, NG, NX, E_, W_, L_, R_, S_ = (t[:, :, :] for t in dts)
                dve.wait_ge(dt_s, 1)
                dve.wait_ge(row_loaded, 48)
                link(V.tensor_tensor(X, X, R_, ALU.add))
                dve.wait_ge(dt_v, 1)
                link(V.tensor_tensor(X, X, over(dbias[:, :], 1, NTOK), ALU.add))
                dve.wait_ge(dt_v, 2)
                link(V.tensor_scalar(NG, X, -1.0, None, ALU.mult))
                dve.wait_ge(dt_v, 3)
                link(V.tensor_tensor(NX, X, NG, ALU.min))
                dve.wait_ge(dt_s, 2)
                link(V.tensor_scalar(W_, E_, 1.0, None, ALU.add))
                dve.wait_ge(dt_v, 5)
                link(V.tensor_scalar(R_, W_, -1.0, None, ALU.add))
                dve.wait_ge(dt_v, 6)
                link(V.scalar_tensor_tensor(S_, R_, 0.0, E_, ALU.is_equal, ALU.mult))
                link(V.tensor_scalar(NG, R_, 2.0 ** -24, None, ALU.max))
                dve.wait_ge(dt_v, 8)
                link(V.reciprocal(R_, NG))
                dve.wait_ge(dt_s, 3)
                link(V.tensor_tensor(L_, L_, E_, ALU.mult))
                dve.wait_ge(dt_v, 10)
                link(V.tensor_tensor(L_, L_, R_, ALU.mult))
                dve.wait_ge(dt_v, 11)
                link(V.tensor_tensor(L_, L_, S_, ALU.add))
                dve.wait_ge(dt_v, 12)
                link(V.scalar_tensor_tensor(dt_[:, :, :], X, 0.0, L_, ALU.max, ALU.add))
                dve.wait_ge(dt_v, 13)
                dve.wait_ge(dt_s, 4)
                V.scalar_tensor_tensor(la[:, :, :], dt_[:, :, :], -1.0, over(alog[:, :], 1, NTOK), ALU.mult,
                                       ALU.mult).then_inc(dt_ready, 1)
                dve.wait_ge(la_hi_ready, 1)
                V.tensor_tensor(la_lo[:, :, :], la[:, :, :], fp(la_hi[:, :, :]), ALU.subtract) \
                    .then_inc(la_lo_ready, 1)

            def dec_chain():
                dve.wait_ge(dec_exp, 1)
                V.tensor_tensor(dtd[:, :], dtd[:, :], dt_[:, 0, :], ALU.mult).then_inc(dt_ready, 1)

            def qk_sums(g, i):
                def f():
                    n = 2 * g + i
                    dve.wait_ge(qk_sq, n + 1)
                    if later(n):
                        dve.wait_ge(qk_rstd, n)
                    V.tensor_reduce(ssum[:, :], sq[:, :, :], AX.X, ALU.add).then_inc(qk_sum, 1)
                    dve.wait_ge(qk_sum, n + 1)
                    V.tensor_scalar(ssum[:, :], ssum[:, :], 1.0 / HD, EPS, ALU.mult, ALU.add).then_inc(qk_ms, 1)
                return f

            def qk_norm(g, i, st):
                def f():
                    n = 2 * g + i
                    dve.wait_ge(qk_rstd, n + 1)
                    v = st[:, :, :].rearrange("p t (h d) -> p (t h) d", d=HD)
                    V.tensor_tensor(v, v, over(rqk[:, :], 2, HD), ALU.mult).then_inc(qk_normed, 1)
                return f

            def at_bias(n, hh):
                def f():
                    dve.wait_ge(scores, n + 1)
                    if hh == 0:
                        dve.wait_ge(slope_done, (n // 4 if isinstance(n, int) else slope_group[0]) + 1)
                    if later(n):
                        dve.wait_ge(p_T, n)
                    V.scalar_tensor_tensor(prob[:, :], dist[:, :], negslope[:, hh:hh + 1], ps[6][:, 0:3 * P],
                                           ALU.mult, ALU.add).then_inc(biased, 1)
                    dve.wait_ge(biased, n + 1)
                    V.tensor_reduce(negmax[:, 0:1], prob[:, 0:T], AX.X, ALU.max, negate=True).then_inc(maxed, 1)
                    V.tensor_reduce(negmax[:, 1:2], prob[:, T:T + P], AX.X, ALU.max, negate=True) \
                        .then_inc(maxed, 1)
                    if hh == 3:
                        V.tensor_scalar(negslope[:, :], negslope[:, :], 0.25, None, ALU.mult) \
                            .then_inc(slope_done, 1)
                return f
            slope_group = [0]

            def at_norm(n):
                def f():
                    dve.wait_ge(expd, n + 1)
                    V.reciprocal(pinv[:, :], psum_[:, :]).then_inc(inv_done, 1)
                    dve.wait_ge(inv_done, n + 1)
                    V.tensor_scalar(prob[:, 0:T], prob[:, 0:T], pinv[:, 0:1], None, ALU.mult).then_inc(normed, 1)
                    V.tensor_scalar(prob[:, T:T + P], prob[:, T:T + P], pinv[:, 1:2], None, ALU.mult) \
                        .then_inc(normed, 1)
                return f

            def at_lo(n):
                def f():
                    dve.wait_ge(aT_hi_done, n + 1)
                    V.tensor_tensor(aT_lo[:, bass.ds(n, 1), :].rearrange("p a t -> p (a t)"), ps[6][:, 0:T],
                                    fp(aT_hi[:, bass.ds(n, 1), :].rearrange("p a t -> p (a t)")),
                                    ALU.subtract).then_inc(aT_lo_done, 1)
                return f

            def attention(n0, g):
                a = [{} for _ in range(3)]
                slope_group[0] = g

                def put(step, f):
                    a[step // 8].setdefault(step % 8, []).append(f)
                for hh in range(4):
                    put(6 * hh, at_bias(n0 + hh, hh))
                    put(6 * hh + 1, at_norm(n0 + hh))
                    put(6 * hh + 4, at_lo(n0 + hh))
                return a

            def add(d, step, f):
                d.setdefault(step, []).append(f)
                return d

            w = {s: [x_lo(XLEAD + s)] for s in range(US - XLEAD)}
            w[5] = [x_mean, dtw_rest]
            steps(B_QKV, w)
            steps(B_QKV + 1, {2: [dt_chain], 4: [qk_sums(0, 0)], 5: [qk_norm(0, 0, q_st)]})
            steps(B_QKV + 2, {1: [qk_sums(0, 1)], 2: [dec_chain], 3: [qk_norm(0, 1, k_st)]})
            def qkv_group(g):
                a = attention(4 * g - 4, g - 1)
                add(a[1], 1, qk_sums(g, 0))
                add(a[1], 3, qk_norm(g, 0, q_st))
                add(a[2], 1, qk_sums(g, 1))
                add(a[2], 3, qk_norm(g, 1, k_st))
                for i in range(3):
                    steps(B_QKV + 3 * g + i, a[i])

            qkv_group(1)
            with dve.Fori(2, 4) as g:
                qkv_group(g)

            def conv_taps(m, half, tap):
                def f():
                    n0 = 12 * m + 6 * half
                    if tap == 0:
                        dve.wait_ge(c_first, 2 * m + half + 1)
                    for tp in ([0], [1, 2])[tap]:
                        for cc in range(2):
                            c = 2 * half + cc
                            sh = tp + 1
                            if tp:
                                dve.wait_ge(c_tap, n0 + 2 * tp - 1 + cc)
                            V.scalar_tensor_tensor(cacc[:, c, sh:T], ps[4 + half][:, cc * T:cc * T + T - sh],
                                                   cw[:, 2 - tp, c:c + 1], cacc[:, c, sh:T], ALU.mult,
                                                   ALU.add).then_inc(c_tap, 1)
                return f

            def conv_work(m, more=None):
                d = dict(more or {})
                add(d, 1, conv_taps(m, 0, 0))
                add(d, 2, conv_taps(m, 0, 1))
                add(d, 3, conv_taps(m, 1, 0))
                add(d, 3, conv_taps(m, 1, 1))
                return d

            a = attention(12, 3)
            steps(B_CONV, a[0])
            steps(B_CONV + 1, conv_work(0, a[1]))
            steps(B_CONV + 2, conv_work(1, a[2]))
            steps(B_CONV + 3, conv_work(2))
            steps(B_CONV + 4, conv_work(3))
            with dve.Fori(0, 3) as i:
                steps(B_CONV + 5 + 2 * i, conv_work(4 + 2 * i))
                steps(B_CONV + 6 + 2 * i, conv_work(5 + 2 * i))
            steps(B_CONV + 11, conv_work(10))

            def xs_at(g, t):
                return xs[:, bass.ds(g, 1), t, :].rearrange("p a n -> p (a n)")

            def ssd_cbm(n):
                def f():
                    dve.wait_ge(cb_mm, n + 1)
                    V.tensor_tensor(cbm[:, :], ps[6][:, 0:P], tri[:, :], ALU.mult).then_inc(cbm_done, 1)
                return f

            def ssd_M(n):
                def f():
                    dve.wait_ge(cbm_done, n + 1)
                    dve.wait_ge(dec_done, 2 * n + 2)
                    V.tensor_tensor(M[:, :, :], M[:, :, :], over(cbm[:, :], 1, HG), ALU.mult) \
                        .then_inc(M_ready, 1)
                return f

            def ssd_y(n, c, g):
                def f():
                    dve.wait_ge(y_mm, n + 1)
                    dve.wait_ge(skip_ready, n + 1)
                    V.tensor_tensor(xs_at(g, c), xs_at(g, c), ps[6][:, :], ALU.add).then_inc(yd_done, 1)
                    if c == 1:
                        dve.wait_ge(off_mm, g + 1)
                        V.tensor_tensor(yoff[:, :, :], heads(ps[7][:, :], HG),
                                        over(eac[:, bass.ds(g * HG, HG)], 2, SHD), ALU.mult).then_inc(yo_done, 1)
                        dve.wait_ge(yo_done, g + 1)
                        dve.wait_ge(yd_done, n + 1)
                        V.tensor_tensor(xs_at(g, c), xs_at(g, c), yoff[:, :, :].rearrange("p h d -> p (h d)"),
                                        ALU.add).then_inc(y_done, 1)
                return f

            def z_gate(g):
                def f():
                    for t in range(NTOK):
                        dve.wait_ge(z_sig, 2 * g + 2)
                        i = V.scalar_tensor_tensor(zs[:, t, :], SETS[0][t][:, :], rstd1[:, t:t + 1], zs[:, t, :],
                                                   ALU.mult, ALU.mult)
                    i.then_inc(set_free[0], 1)
                return f

            def y_gated(g, k):
                def f():
                    dve.wait_ge(y_done, g + 1)
                    dve.wait_ge(set_free[0], 11 + g)
                    v = xs[:, bass.ds(g, 1), :, :].rearrange("p a t n -> p (a t) n")
                    V.tensor_tensor(v, v, zs[:, :, :], ALU.mult).then_inc(yz_done, 1)
                return f

            def y_norm(g):
                def f():
                    dve.wait_ge(ysq_done, 2 * g + 2)
                    if later(g):
                        dve.wait_ge(yrs_done, g)
                    V.tensor_scalar(gss[:, :], gss[:, :], 1.0 / GW, EPS, ALU.mult, ALU.add).then_inc(yms_done, 1)
                    dve.wait_ge(yrs_done, g + 1)
                    for t in range(NTOK):
                        V.tensor_scalar(xs_at(g, t), xs_at(g, t), grs[:, t:t + 1], None, ALU.mult) \
                            .then_inc(yfin, 1)
                return f

            def merge_attn(b, j):
                def f():
                    block_done(b)
                    dve.wait_ge(set_free[1], 11 + 2 * j)
                    for t in range(NTOK):
                        v = merged[:, t, bass.ds(j * COLS, COLS)]
                        i = V.tensor_tensor(v, v, SETS[1][t][:, :], ALU.mult)
                    i.then_inc(set_free[1], 1)
                return f

            def ssd_blocks(j):
                b = B_SSD + 4 * j
                n = 4 * j
                g = 2 * j
                if later(j):
                    steps(b, {1: [ssd_cbm(n)], 3: [ssd_M(n)], 5: [ssd_y(n, 0, g)], 7: [z_gate(g)]})
                else:
                    steps(b, {1: [conv_taps(11, 0, 0), conv_taps(11, 0, 1)],
                              2: [conv_taps(11, 1, 0), conv_taps(11, 1, 1)],
                              6: [ssd_cbm(n)], 7: [ssd_M(n), z_gate(g), ssd_y(n, 0, g)]})
                steps(b + 1, {1: [ssd_cbm(n + 1)], 3: [ssd_M(n + 1)], 5: [ssd_y(n + 1, 1, g)],
                              6: [y_gated(g, 0)], 7: [y_norm(g)]})
                steps(b + 2, {1: [ssd_cbm(n + 2)], 3: [ssd_M(n + 2)], 5: [ssd_y(n + 2, 0, g + 1)],
                              7: [z_gate(g + 1)]})
                steps(b + 3, {1: [ssd_cbm(n + 3)], 3: [ssd_M(n + 3)], 5: [ssd_y(n + 3, 1, g + 1)],
                              6: [y_gated(g + 1, 1)], 7: [y_norm(g + 1), merge_attn(b + 3, j)]})

            ssd_blocks(0)
            with dve.Fori(1, 4) as j:
                ssd_blocks(j)

            def s_lo(G, i):
                def f():
                    for half in range(2):
                        dve.wait_ge(sT_hi_done, 4 * G + 2 * half + 2)
                        for cc in range(2):
                            c = 2 * half + cc
                            V.scalar_tensor_tensor(
                                sT_lo[:, bass.ds(4 * G + c, 1), :].rearrange("p a t -> p (a t)"),
                                ps[4 + 2 * i + half][:, cc * T:(cc + 1) * T], sw[i][:, c:c + 1],
                                fp(sT_hi[:, bass.ds(4 * G + c, 1), :].rearrange("p a t -> p (a t)")),
                                ALU.mult, ALU.subtract).then_inc(sT_lo_done, 1)
                return f

            with dve.Fori(0, 4) as jb:
                steps(B_GATE + jb, {2: [s_lo(2 * jb, 0)], 6: [s_lo(2 * jb + 1, 1)]})

            def merge_ssm(j):
                def f():
                    block_done(B_SSM + 2 * j + 1)
                    dve.wait_ge(set_free[0], 21 + j)
                    if later(j):
                        dve.wait_ge(m_T, j)
                    for t in range(NTOK):
                        V.tensor_tensor(m_st[:, t, :], SETS[1][t][:, :], s_half[:, t, :], ALU.add) \
                            .then_inc((m_step, set_free[1])[t], 1)
                    for t in range(NTOK):
                        dve.wait_ge((m_step, set_free[1])[t], (3 * j + 1, 21 + j)[t])
                        V.tensor_tensor(m_st[:, t, :], m_st[:, t, :], sgate[:, t, bass.ds(j * COLS, COLS)],
                                        ALU.mult).then_inc(m_step, 1)
                return f

            def g_lo(j):
                def f():
                    for i in range(2):
                        dve.wait_ge(gT_hi_done, 2 * j + i + 1)
                        V.tensor_tensor(gT_lo[:, bass.ds(4 * j + 2 * i, 2), :], heads(ps[4 + i][:, :], 2),
                                        fp(gT_hi[:, bass.ds(4 * j + 2 * i, 2), :]), ALU.subtract) \
                            .then_inc(gT_lo_done, 1)
                return f

            steps(B_SSM)
            steps(B_SSM + 1, {7: [merge_ssm(0)]})
            with dve.Fori(1, 4) as j:
                steps(B_SSM + 2 * j, {3: [g_lo(j - 1)]})
                steps(B_SSM + 2 * j + 1, {7: [merge_ssm(j)]})

            def h_add(j):
                def f():
                    block_done(B_OUT + j)
                    dve.wait_ge(x_again, 16)
                    for t in range(NTOK):
                        v = h[:, t, j * COLS:(j + 1) * COLS]
                        i = V.tensor_tensor(v, v, SETS[j % 2][t][:, :], ALU.add)
                    i.then_inc(set_free[j % 2], 1)
                return f

            def h_lo(j):
                def f():
                    ba = 6 if j % 2 == 0 else 4
                    for half in range(2):
                        dve.wait_ge(hT_hi_done, 4 * j + 2 * half + 2)
                        for cc in range(2):
                            kt = 4 * j + 2 * half + cc
                            V.scalar_tensor_tensor(hT_lo[:, kt, :], ps[ba + half][:, cc * T:(cc + 1) * T],
                                                   par[:, MLP_C + kt:MLP_C + kt + 1], fp(hT_hi[:, kt, :]),
                                                   ALU.mult, ALU.subtract).then_inc(hT_lo_done, 1)
                return f

            steps(B_OUT, {2: [g_lo(3)], 7: [h_add(0)]})
            for j in range(1, 4):
                steps(B_OUT + j, {2: [h_lo(j - 1)], 7: [h_add(j)]})

            def h_mean():
                dve.wait_ge(h_sq, 8)
                V.tensor_reduce(hs2[:, :], hss[:, :, :], AX.X, ALU.add).then_inc(hsum_done, 1)
                dve.wait_ge(hsum_done, 1)
                V.tensor_scalar(hs2[:, :], hs2[:, :], 1.0 / D, EPS, ALU.mult, ALU.add).then_inc(hms_done, 1)

            def f_lo(n, u):
                def f():
                    for i in range(2):
                        dve.wait_ge(fT_hi_done, 2 * n + i + 1)
                        V.tensor_tensor(fT_lo[:, 4 * u + 2 * i:4 * u + 2 * i + 2, :],
                                        heads(ps[4 + 2 * (u % 2) + i][:, :], 2),
                                        fp(fT_hi[:, 4 * u + 2 * i:4 * u + 2 * i + 2, :]), ALU.subtract) \
                            .then_inc(fT_lo_done, 1)
                return f

            def h_down(q, d, last=False):
                def f():
                    block_done(B_MLP + 8 * q + 4 + d)
                    for t in range(NTOK):
                        v = h[:, t, d * COLS:(d + 1) * COLS]
                        i = V.tensor_tensor(v, v, SETS[d % 2][t][:, :], ALU.add)
                        if last and t == 0:
                            i.then_inc(last_tile0, 1)
                    i.then_inc(set_free[d % 2], 1)
                return f

            def mlp(q, end=False):
                b = B_MLP + 8 * q
                for u in range(4):
                    if later(q) or u:
                        steps(b + u, {3: [f_lo(4 * q + u - 1, u - 1)]} if u else None)
                    else:
                        steps(b, {1: [h_lo(3)], 2: [h_mean]})
                steps(b + 4, {3: [f_lo(4 * q + 3, 3)], 7: [h_down(q, 0)]})
                for d in range(1, 4):
                    steps(b + 4 + d, {7: [h_down(q, d, end and d == 3)]}, last=end and d == 3)

            mlp(0)
            with dve.Fori(1, 3) as q:
                mlp(q)
            mlp(3, end=True)

        @block.gpsimd
        def _(pool):
            G = nc.gpsimd
            G.memset(ident[:, :], 0.0).then_inc(const_step, 1)
            G.memset(tri[:, :], 1.0).then_inc(const_step, 1)
            G.memset(strict[:, :], 1.0).then_inc(const_step, 1)
            pool.wait_ge(const_step, 3)
            G.affine_select(out=ident[:, :], in_=ident[:, :], compare_op=ALU.not_equal, fill=1.0, base=0,
                            pattern=[[-1, P]], channel_multiplier=1)
            G.affine_select(out=tri[:, :], in_=tri[:, :], compare_op=ALU.is_ge, fill=0.0, base=0,
                            pattern=[[1, P]], channel_multiplier=-1)
            G.affine_select(out=strict[:, :], in_=strict[:, :], compare_op=ALU.is_ge, fill=0.0, base=-1,
                            pattern=[[-1, P]], channel_multiplier=1).then_inc(const_ready, 1)
            for hh in range(4):
                G.memset(negslope[:, hh:hh + 1], -(2.0 ** (-8.0 * (hh + 1) / NH)))
            G.memset(neghalf[:, :], -0.5)
            G.iota(dist_i[:, 0:P], pattern=[[-1, P]], base=P, channel_multiplier=1)
            G.iota(dist_i[:, P:3 * P], pattern=[[0, 2], [-1, P]], base=0, channel_multiplier=1).then_inc(const_step, 1)
            pool.wait_ge(const_step, 4)
            G.tensor_copy(dist[:, :], dist_i[:, :]).then_inc(const_step, 1)
            pool.wait_ge(const_step, 5)
            G.affine_select(out=dist[:, P:3 * P], in_=dist[:, P:3 * P], compare_op=ALU.is_ge, fill=1e33, base=0,
                            pattern=[[0, 2], [-1, P]], channel_multiplier=1).then_inc(slope_done, 1)
            pool.wait_ge(slope_done, 1)
            pool.wait_ge(par_ready, 1)
            G.tensor_scalar(par[:, QN_C:QN_C + 1], par[:, QN_C:QN_C + 1], HD ** -0.5, None, ALU.mult) \
                .then_inc(const_ready, 1)
            pool.wait_ge(xms_done, 1)
            G.tensor_tensor(rstd1[:, :], xss[:, :], neghalf[:, 0:2], ALU.pow).then_inc(rstd1_ready, 1)

            def qk_work(g, i, st):
                n = 2 * g + i
                pool.wait_ge(set_free[i], g + 1)
                if later(n):
                    pool.wait_ge(qk_sum, n)
                v = st[:, :, :].rearrange("p t (h d) -> p (t h) d", d=HD)
                G.tensor_tensor(sq[:, :, :], v, v, ALU.mult).then_inc(qk_sq, 1)
                pool.wait_ge(qk_ms, n + 1)
                if later(n):
                    pool.wait_ge(qk_normed, n)
                G.tensor_tensor(rqk[:, :], ssum[:, :], neghalf[:, :], ALU.pow).then_inc(qk_rstd, 1)

            pool.wait_ge(dt_ready, 1)
            qk_work(0, 0, q_st)
            qk_work(0, 1, k_st)
            with pool.Fori(1, 4) as g:
                qk_work(g, 0, q_st)
                qk_work(g, 1, k_st)

            def conv_par(m, cb_):
                if later(m):
                    pool.wait_ge(c_tap, 12 * m)
                G.tensor_copy(cb[:, :], par[:, bass.ds(CB_C + 4 * cb_, 4)])
                for k in range(4):
                    i = G.tensor_copy(cw[:, k, :], par[:, bass.ds(CW_C + 48 * k + 4 * cb_, 4)])
                i.then_inc(c_par, 1)

            for m in range(4):
                conv_par(m, 8 + m)
            with pool.Fori(0, 8) as m:
                conv_par(4 + m, m)

            def ssd(n, c, g):
                if later(n):
                    pool.wait_ge(y_mm, n)
                xg = heads(xs[:, bass.ds(g, 1), c, :].rearrange("p a n -> p (a n)"), HG)
                if c == 0:
                    G.tensor_copy(BTg[:, :], BT[:, bass.ds(g, 1), :].rearrange("p a t -> p (a t)"))
                    G.tensor_copy(CTg[:, :], CT[:, bass.ds(g, 1), :].rearrange("p a t -> p (a t)"))
                    G.tensor_copy(Btg[:, :], Btok[:, bass.ds(g * NST, NST)]).then_inc(g_copied, 1)
                G.tensor_tensor(tla_hi[:, :, :], over(tri[:, :], 1, HG),
                                over(fp(la_hi[:, c, bass.ds(g * HG, HG)]), 2, P),
                                ALU.mult)
                G.tensor_tensor(tla_lo[:, :, :], over(tri[:, :], 1, HG),
                                over(fp(la_lo[:, c, bass.ds(g * HG, HG)]), 2, P),
                                ALU.mult).then_inc(tla_ready, 1)
                if c == 0:
                    G.tensor_tensor(xd[:, :, :], xg, over(dtd[:, bass.ds(g * HG, HG)], 2, SHD), ALU.mult)
                G.tensor_tensor(xf[:, :, :], xg, over(dt_[:, c, bass.ds(g * HG, HG)], 2, SHD), ALU.mult) \
                    .then_inc(xf_ready, 1)
                G.tensor_tensor(xg, xg, over(dskip[:, bass.ds(g * HG, HG)], 2, SHD), ALU.mult) \
                    .then_inc(skip_ready, 1)

            def y_rstd(g):
                pool.wait_ge(yms_done, g + 1)
                if later(g):
                    pool.wait_ge(yfin, 2 * g)
                G.tensor_tensor(grs[:, :], gss[:, :], neghalf[:, 0:2], ALU.pow).then_inc(yrs_done, 1)

            pool.wait_ge(c_out, 3)
            pool.wait_ge(c_silu, 5)
            pool.wait_ge(dt_ready, 2)
            pool.wait_ge(la_lo_ready, 1)
            def ssd_groups(j):
                ssd(4 * j, 0, 2 * j)
                if later(j):
                    y_rstd(2 * j - 1)
                ssd(4 * j + 1, 1, 2 * j)
                ssd(4 * j + 2, 0, 2 * j + 1)
                y_rstd(2 * j)
                ssd(4 * j + 3, 1, 2 * j + 1)

            ssd_groups(0)
            pool.wait_ge(c_out, 10)
            with pool.Fori(1, 4) as j:
                ssd_groups(j)
            y_rstd(7)

            def y_copy(Gn, i):
                pool.wait_ge(yfin, 2 * Gn + 2)
                G.tensor_copy(y_st[i][:, :, :], xs[:, bass.ds(Gn, 1), :, :].rearrange("p a t n -> p (a t) n"))
                G.tensor_copy(sw[i][:, :], par[:, bass.ds(SSM_C + 4 * Gn, 4)]).then_inc(y_copied, 1)

            pool.wait_ge(y_mm, 16)
            pool.wait_ge(yz_done, 8)
            y_copy(0, 0)
            y_copy(1, 1)
            with pool.Fori(1, 4) as j:
                for i in range(2):
                    pool.wait_ge(sT_lo_done, 8 * j - 4 + 4 * i)
                    y_copy(2 * j + i, i)

            with pool.Fori(0, 4) as j:
                pool.wait_ge(m_step, 3 * j + 3)
                G.tensor_tensor(m_st[:, :, :], m_st[:, :, :], merged[:, :, bass.ds(j * COLS, COLS)], ALU.add) \
                    .then_inc(m_ready, 1)
            pool.wait_ge(hms_done, 1)
            G.tensor_tensor(rstd2[:, :], hs2[:, :], neghalf[:, 0:2], ALU.pow).then_inc(rstd2_ready, 1)
            with pool.Fori(0, 4) as q:
                for u in range(4):
                    pool.wait_ge(set_free[u % 2], 27 + 4 * q + u // 2)
                    G.tensor_tensor(r_st[:, :, :], r_st[:, :, :], r_st[:, :, :], ALU.mult).then_inc(r_ready, 1)


_INS = ["x", "mix_norm_w", "w_in", "q_norm_w", "k_norm_w", "conv_w", "conv_b", "dt_bias", "a_log", "d_skip",
        "ssm_norm_w", "w_attn_out", "w_ssm_out", "w_out", "mlp_norm_w", "w_up", "w_down"]


def kernel(**inputs):
    import numpy as np
    import concourse.bacc as bacc
    from concourse.bass_utils import run_bass_kernel_spmd

    nc = bacc.Bacc("TRN2", target_bir_lowering=False, num_devices=1)
    arrays, args = {}, []
    for name in _INS:
        a = np.ascontiguousarray(inputs[name])
        arrays[f"in_{name}"] = a
        args.append(nc.dram_tensor(f"in_{name}", a.shape, mybir.dt.from_np(a.dtype), kind="ExternalInput").ap())
    args.append(nc.dram_tensor("out_h", (1, T, D), mybir.dt.float32, kind="ExternalOutput").ap())
    build(nc, *args)
    r = run_bass_kernel_spmd(nc, [arrays], core_ids=[0])
    return r.results[0]["out_h"]
```
